# Optimizing a Trainium2 kernel written in Bass

```python
import jax
import jax.numpy as jnp
from jax import lax
import numpy as np

D_MODEL = 1024
BATCH = 1
SEQ = 2048
DEPTH = 2
DEC_BATCH = 8
DEC_SEQ = 8
PAST_LEN = 8192
PAGE_SIZE = 128

SB_HEADS = 8
SB_HEAD_DIM = 64
SB_WIDTH = SB_HEADS * SB_HEAD_DIM
SB_BLOCK = 128
SB_BIAS_INIT = -6.0
GDN_HEADS = 4
GDN_DK = 128
GDN_DV = 128
GDN_QK_WIDTH = GDN_HEADS * GDN_DK
GDN_V_WIDTH = GDN_HEADS * GDN_DV
GDN_QKV_WIDTH = 2 * GDN_QK_WIDTH + GDN_V_WIDTH
GDN_CONV = 4
GDN_CHUNK = 64
SC_WIDTH = D_MODEL
SC_CONV = 3
AB_IN_COLS = 4 * SB_WIDTH + GDN_QKV_WIDTH + GDN_V_WIDTH + 2 * GDN_HEADS
AB_MIX_WIDTH = SB_WIDTH + GDN_V_WIDTH
L_AB = (DEPTH + 1) // 2
L_C = DEPTH // 2
NORM_EPS = 1e-6

kernel_name = "stickbreak_gdn_shortconv_hybrid_step"

def rms_norm(x, w):
    xf = x.astype(jnp.float32)
    y = xf * lax.rsqrt(jnp.mean(xf * xf, axis=-1, keepdims=True) + NORM_EPS)
    return (y * w.astype(jnp.float32)).astype(x.dtype)

def l2norm(x):
    xf = x.astype(jnp.float32)
    return xf * lax.rsqrt(jnp.sum(xf * xf, axis=-1, keepdims=True) + NORM_EPS)

def causal_conv(x, buf, w):
    t = x.shape[1]
    width = w.shape[0]
    xx = jnp.concatenate([buf.astype(x.dtype), x], axis=1)
    y = xx[:, 0:t] * w[0]
    for i in range(1, width):
        y = y + xx[:, i:i + t] * w[i]
    return y, xx[:, t:]

def stick_breaking_attention(q, k, v, bias, q_offset):
    n, t, h, d = q.shape
    s_len = k.shape[1]
    qb = min(SB_BLOCK, t)
    nb = t // qb
    scale = d ** -0.5
    q_blocks = jnp.moveaxis(q.astype(jnp.float32).reshape(n, nb, qb, h, d), 1, 0)
    kf = k.astype(jnp.float32)
    vf = v.astype(jnp.float32)
    bf = bias.astype(jnp.float32)[None, :, None, None]
    key_pos = jnp.arange(s_len)

    def block(args):
        q_blk, start = args
        z = jnp.einsum('nqhd,nshd->nhqs', q_blk, kf) * scale + bf
        q_pos = q_offset + start + jnp.arange(qb)
        mask = key_pos[None, :] < q_pos[:, None]
        log_1m = jnp.where(mask, jax.nn.log_sigmoid(-z), 0.0)
        log_rest = lax.cumsum(log_1m, axis=3, reverse=True) - log_1m
        a = jnp.where(mask, jnp.exp(jax.nn.log_sigmoid(z) + log_rest), 0.0)
        return jnp.einsum('nhqs,nshd->nqhd', a, vf)

    out = lax.map(block, (q_blocks, jnp.arange(nb) * qb))
    return jnp.moveaxis(out, 0, 1).reshape(n, t, h, d).astype(q.dtype)

def gated_delta_rule(q, k, v, g, beta, state):
    f32 = jnp.float32
    n, t, h, dk = q.shape
    dv = v.shape[-1]
    c = min(GDN_CHUNK, t)
    pad = (-t) % c
    q, k, v, g, beta = [jnp.pad(a.astype(f32), [(0, 0), (0, pad)] + [(0, 0)] * (a.ndim - 2))
                        for a in (q, k, v, g, beta)]
    nc = (t + pad) // c

    def chunked(a):
        return jnp.moveaxis(a.reshape((n, nc, c, h) + a.shape[3:]), 3, 1)

    q, k, v, g, beta = [chunked(a) for a in (q, k, v, g, beta)]
    g_cum = jnp.cumsum(g, axis=-1)
    idx = jnp.arange(c)
    causal = idx[:, None] >= idx[None, :]
    strict = idx[:, None] > idx[None, :]
    decay = jnp.exp(jnp.where(causal, g_cum[..., :, None] - g_cum[..., None, :], -jnp.inf))
    k_beta = k * beta[..., None]
    m = jnp.where(strict, jnp.einsum('nhcid,nhcjd->nhcij', k_beta, k) * decay, 0.0)
    eye = jnp.eye(c, dtype=f32)
    t_inv = lax.linalg.triangular_solve(m + eye, jnp.broadcast_to(eye, m.shape),
                                        left_side=True, lower=True, unit_diagonal=True)
    u = t_inv @ (v * beta[..., None])
    w = t_inv @ (k_beta * jnp.exp(g_cum)[..., None])
    qk = jnp.where(causal, jnp.einsum('nhcid,nhcjd->nhcij', q, k) * decay, 0.0)

    def step(s, xs):
        q_c, k_c, u_c, w_c, qk_c, g_c = xs
        v_new = u_c - w_c @ s
        o_c = (q_c * jnp.exp(g_c)[..., None]) @ s + qk_c @ v_new
        g_last = g_c[..., -1:]
        s = s * jnp.exp(g_last)[..., None] + jnp.einsum(
            'nhck,nhcv->nhkv', k_c * jnp.exp(g_last - g_c)[..., None], v_new)
        return s, o_c

    xs = tuple(jnp.moveaxis(a, 2, 0) for a in (q, k, u, w, qk, g_cum))
    state, o = lax.scan(step, state.astype(f32), xs)
    o = jnp.moveaxis(jnp.moveaxis(o, 0, 2), 1, 3).reshape(n, nc * c, h, dv)[:, :t]
    return o, state

def ab_mixer(xn, w_in, sb_bias, conv_w, a_log, dt_bias, out_norm_w, w_out,
             past_k, past_v, q_offset, gdn_state, gdn_buf):
    n, t, _ = xn.shape
    sizes = [SB_WIDTH] * 4 + [GDN_QKV_WIDTH, GDN_V_WIDTH, GDN_HEADS, GDN_HEADS]
    splits = [int(s) for s in np.cumsum(sizes)[:-1]]
    proj = jnp.einsum('ntd,dc->ntc', xn, w_in)
    sb_q, sb_k, sb_v, sb_z, g_qkv, g_z, g_b, g_a = jnp.split(proj, splits, axis=-1)
    q = sb_q.reshape(n, t, SB_HEADS, SB_HEAD_DIM)
    k = sb_k.reshape(n, t, SB_HEADS, SB_HEAD_DIM)
    v = sb_v.reshape(n, t, SB_HEADS, SB_HEAD_DIM)
    if past_k is None:
        keys, vals = k, v
    else:
        keys = jnp.concatenate([past_k.astype(k.dtype), k], axis=1)
        vals = jnp.concatenate([past_v.astype(v.dtype), v], axis=1)
    o_a = stick_breaking_attention(q, keys, vals, sb_bias, q_offset).reshape(n, t, SB_WIDTH) * jax.nn.silu(sb_z)
    qkv, new_buf = causal_conv(g_qkv, gdn_buf, conv_w)
    qkv = jax.nn.silu(qkv)
    gq, gk, gv = jnp.split(qkv, [GDN_QK_WIDTH, 2 * GDN_QK_WIDTH], axis=-1)
    gq = l2norm(gq.reshape(n, t, GDN_HEADS, GDN_DK)) * (GDN_DK ** -0.5)
    gk = l2norm(gk.reshape(n, t, GDN_HEADS, GDN_DK))
    gv = gv.reshape(n, t, GDN_HEADS, GDN_DV)
    beta = jax.nn.sigmoid(g_b.astype(jnp.float32))
    g = -jnp.exp(a_log.astype(jnp.float32)) * jax.nn.softplus(
        g_a.astype(jnp.float32) + dt_bias.astype(jnp.float32))
    o_b, new_state = gated_delta_rule(gq, gk, gv, g, beta, gdn_state)
    o_b = rms_norm(o_b, out_norm_w).astype(xn.dtype).reshape(n, t, GDN_V_WIDTH) * jax.nn.silu(g_z)
    out = jnp.einsum('ntc,cd->ntd', jnp.concatenate([o_a, o_b], axis=-1), w_out)
    return out, k, v, new_state, new_buf

def sconv_mixer(xn, w_in, conv_w, w_out, conv_buf):
    proj = jnp.einsum('ntd,dc->ntc', xn, w_in)
    u, gate_b, gate_c, z = jnp.split(proj, 4, axis=-1)
    y, new_buf = causal_conv(gate_c * u, conv_buf, conv_w)
    out = jnp.einsum('ntc,cd->ntd', gate_b * y * jax.nn.silu(z), w_out)
    return out, new_buf

def gather_pages(pool, page_table):
    rows = pool[page_table]
    return rows.reshape(page_table.shape[0], page_table.shape[1] * pool.shape[1], pool.shape[2], pool.shape[3])

def run_trunk(x, pool_k, pool_v, page_table, gdn_state, gdn_buf, sc_buf,
              norm_w, ab_w_in, ab_sb_bias, ab_conv_w, ab_a_log, ab_dt_bias, ab_out_norm_w, ab_w_out,
              sc_w_in, sc_conv_w, sc_w_out, final_norm_w):
    h = x
    q_offset = 0 if page_table is None else page_table.shape[1] * pool_k.shape[2]
    new_k, new_v, new_s, new_gbuf, new_scbuf = [], [], [], [], []
    for layer in range(DEPTH):
        xn = rms_norm(h, norm_w[layer])
        i = layer // 2
        if layer % 2 == 0:
            if page_table is None:
                pk = pv = None
            else:
                pk = gather_pages(pool_k[i], page_table)
                pv = gather_pages(pool_v[i], page_table)
            out, k_rows, v_rows, s_i, buf_i = ab_mixer(
                xn, ab_w_in[i], ab_sb_bias[i], ab_conv_w[i], ab_a_log[i], ab_dt_bias[i], ab_out_norm_w[i],
                ab_w_out[i], pk, pv, q_offset, gdn_state[i], gdn_buf[i])
            new_k.append(k_rows)
            new_v.append(v_rows)
            new_s.append(s_i.astype(gdn_state.dtype))
            new_gbuf.append(buf_i)
        else:
            out, buf_i = sconv_mixer(xn, sc_w_in[i], sc_conv_w[i], sc_w_out[i], sc_buf[i])
            new_scbuf.append(buf_i)
        h = h + out
    y = rms_norm(h, final_norm_w)
    return y, jnp.stack(new_k), jnp.stack(new_v), jnp.stack(new_s), jnp.stack(new_gbuf), jnp.stack(new_scbuf)

def setup_inputs(seed: int = 0) -> dict:
    key = jax.random.key(seed)
    ks = jax.random.split(key, 24)
    f32 = jnp.float32
    n_pages = PAST_LEN // PAGE_SIZE
    n_used = DEC_BATCH * n_pages
    n_pool = n_used + max(1, n_used // 4)
    page_table = jax.random.permutation(ks[0], n_pool)[:n_used].reshape(DEC_BATCH, n_pages).astype(jnp.int32)
    dt = jnp.exp(jax.random.uniform(ks[1], (L_AB, GDN_HEADS), f32, np.log(1e-3), np.log(1e-1)))
    return {
        "x_prompt": jax.random.normal(ks[2], (BATCH, SEQ, D_MODEL), f32),
        "x_sample": jax.random.normal(ks[3], (DEC_BATCH, DEC_SEQ, D_MODEL), f32),
        "cache_sb_k": jax.random.normal(ks[4], (L_AB, n_pool, PAGE_SIZE, SB_HEADS, SB_HEAD_DIM), f32),
        "cache_sb_v": jax.random.normal(ks[5], (L_AB, n_pool, PAGE_SIZE, SB_HEADS, SB_HEAD_DIM), f32),
        "state_gdn": jax.random.normal(ks[6], (L_AB, DEC_BATCH, GDN_HEADS, GDN_DK, GDN_DV), f32) * GDN_DK ** -0.5,
        "state_gdn_conv": jax.random.normal(ks[7], (L_AB, DEC_BATCH, GDN_CONV - 1, GDN_QKV_WIDTH), f32),
        "state_sconv": jax.random.normal(ks[8], (L_C, DEC_BATCH, SC_CONV - 1, SC_WIDTH), f32),
        "page_table": page_table,
        "norm_w": 1.0 + 0.02 * jax.random.normal(ks[9], (DEPTH, D_MODEL), f32),
        "ab_w_in": jax.random.normal(ks[10], (L_AB, D_MODEL, AB_IN_COLS), f32) * D_MODEL ** -0.5,
        "ab_sb_bias": SB_BIAS_INIT + 0.5 * jax.random.normal(ks[19], (L_AB, SB_HEADS), f32),
        "ab_conv_w": jax.random.normal(ks[11], (L_AB, GDN_CONV, GDN_QKV_WIDTH), f32) * GDN_CONV ** -0.5,
        "ab_a_log": jnp.log(jax.random.uniform(ks[12], (L_AB, GDN_HEADS), f32, 1.0, 16.0)),
        "ab_dt_bias": dt + jnp.log(-jnp.expm1(-dt)),
        "ab_out_norm_w": 1.0 + 0.02 * jax.random.normal(ks[13], (L_AB, GDN_DV), f32),
        "ab_w_out": jax.random.normal(ks[14], (L_AB, AB_MIX_WIDTH, D_MODEL), f32) * AB_MIX_WIDTH ** -0.5,
        "sc_w_in": jax.random.normal(ks[15], (L_C, D_MODEL, 4 * SC_WIDTH), f32) * D_MODEL ** -0.5,
        "sc_conv_w": jax.random.normal(ks[16], (L_C, SC_CONV, SC_WIDTH), f32) * SC_CONV ** -0.5,
        "sc_w_out": jax.random.normal(ks[17], (L_C, SC_WIDTH, D_MODEL), f32) * SC_WIDTH ** -0.5,
        "final_norm_w": 1.0 + 0.02 * jax.random.normal(ks[18], (D_MODEL,), f32),
    }

def reference(x_prompt, x_sample, cache_sb_k, cache_sb_v, state_gdn, state_gdn_conv, state_sconv, page_table,
              norm_w, ab_w_in, ab_sb_bias, ab_conv_w, ab_a_log, ab_dt_bias, ab_out_norm_w, ab_w_out,
              sc_w_in, sc_conv_w, sc_w_out, final_norm_w):
    weights = (norm_w, ab_w_in, ab_sb_bias, ab_conv_w, ab_a_log, ab_dt_bias, ab_out_norm_w, ab_w_out,
               sc_w_in, sc_conv_w, sc_w_out, final_norm_w)
    nb = x_prompt.shape[0]
    dt = x_prompt.dtype
    p_gdn = jnp.zeros((L_AB, nb, GDN_HEADS, GDN_DK, GDN_DV), dt)
    p_gbuf = jnp.zeros((L_AB, nb, GDN_CONV - 1, GDN_QKV_WIDTH), dt)
    p_scbuf = jnp.zeros((L_C, nb, SC_CONV - 1, SC_WIDTH), dt)
    y_prompt, k_p, v_p, s_p, gb_p, sc_p = run_trunk(
        x_prompt, None, None, None, p_gdn, p_gbuf, p_scbuf, *weights)
    y_sample, k_s, v_s, s_s, gb_s, sc_s = run_trunk(
        x_sample, cache_sb_k, cache_sb_v, page_table, state_gdn, state_gdn_conv, state_sconv, *weights)
    return (y_prompt, y_sample, k_p, v_p, k_s, v_s, s_p, s_s, gb_p, gb_s, sc_p, sc_s)


_drawn_inputs = setup_inputs


def setup_inputs(seed=0):
    import zlib

    import numpy as np

    out = dict(_drawn_inputs(seed))
    spreads = {}
    factors = {'ab_sb_bias': 36.608,
     'ab_out_norm_w': 5.01,
     'final_norm_w': 8.407,
     'cache_sb_k': 8.0,
     'cache_sb_v': 8.0}
    for name, (base, spread) in spreads.items():
        noise = np.random.default_rng([zlib.crc32(name.encode()), seed]).standard_normal(out[name].shape)
        drawn = base * np.exp(spread * noise) if base else spread * noise
        out[name] = jnp.asarray(drawn.astype(out[name].dtype))
    for name, factor in factors.items():
        out[name] = (out[name] * factor).astype(out[name].dtype)
    return out
```

```python
from contextlib import ExitStack

import numpy as np

import concourse.bass as bass
from concourse import mybir

F32 = mybir.dt.float32
F32R = mybir.dt.float32r
I32 = mybir.dt.int32
ACT = mybir.ActivationFunctionType
ALU = mybir.AluOpType
ds = bass.ds

P = 128
D = 1024
KC = D // P
SEQ = 2048
NS, TS = 8, 8
T = SEQ + NS * TS
NG = 6
GW = T // NG
assert GW * NG == T and GW <= 512
EPS = 1e-6
SBH, SBD = 8, 64
GH = 4
PAGE = 128
NPAGE = 64
Q0, K0, V0, BA0, Z0, GZ0, NROW = 0, 4, 8, 12, 13, 17, 21


class Stage:

    def __init__(self, nc, name):
        self.nc, self.name, self.ctx, self.sems = nc, name, ExitStack(), []

    def __enter__(self):
        return self

    def __exit__(self, *a):
        self.ctx.__exit__(*a)
        self.nc.clear_and_free_semaphores(self.sems)
        self.nc.all_engine_barrier()

    def sb(self, name, shape, dt=F32):
        return self.ctx.enter_context(self.nc.sbuf_tensor(f"{self.name}_{name}", shape, dt))

    def psum(self, name, shape):
        return self.ctx.enter_context(self.nc.psum_tensor(f"{self.name}_{name}", shape, F32))

    def sem(self, name):
        self.sems.append(self.nc.alloc_semaphore(f"{self.name}_{name}"))
        return self.sems[-1]

    def block(self):
        return self.ctx.enter_context(self.nc.Block())


def norm(nc, name, src, w_dram, xh, xl, dst):
    with Stage(nc, name) as st:
        x = st.sb("x", [P, 2, KC, GW])
        sq = st.sb("sq", [P, 2, KC, GW])
        root = st.sb("root", [P, 2, GW])
        rstd = st.sb("rstd", [P, 2, GW])
        w = st.sb("w", [P, KC])
        mean = st.sb("mean", [P, P])
        ss = st.psum("ss", [P, 2, 512])
        w_in, mean_set = st.sem("w_in"), st.sem("mean_set")
        x_in = [st.sem(f"x_in{b}") for b in range(2)]
        x_free = st.sem("x_free")
        squared, summed, scaled, rounded = st.sem("squared"), st.sem("summed"), st.sem("scaled"), st.sem("rounded")
        stored, rooted, eps_set = st.sem("stored"), st.sem("rooted"), st.sem("eps_set")
        eps = st.sb("eps", [P, 1])
        block = st.block()
        to_sbuf = dst is None
        src_v = src.rearrange("(c p) t -> p c t", p=P)

        @block.sync
        def _(sp):
            sp.dma_start(w[:], w_dram).then_inc(w_in, 16)
            with sp.Fori(0, NG // 2) as i:
                for b in range(2):
                    sp.wait_ge(x_free, i * 2 + b + 1)
                    sp.dma_start(x[:, b], src_v[:, :, ds((i * 2 + b) * GW, GW)]).then_inc(x_in[b], 16)
                    if not to_sbuf:
                        sp.wait_ge(scaled, i * 2 + b + 1)
                        sp.dma_start(dst.rearrange("(c p) t -> p c t", p=P)[:, :, ds((i * 2 + b) * GW, GW)],
                                     x[:, b]).then_inc(stored, 16)
            if not to_sbuf:
                sp.wait_ge(stored, 16 * NG)

        @block.scalar
        def _(act):
            if not to_sbuf:
                act.sem_inc(x_free, 2)
            act.wait_ge(eps_set, 1)
            with act.Fori(0, NG // 2) as i:
                for b in range(2):
                    act.wait_ge(x_in[b], i * 16 + 16)
                    nc.scalar.activation(sq[:, b], x[:, b], ACT.Square).then_inc(squared, 1)
                    act.wait_ge(summed, i * 2 + b + 1)
                    nc.scalar.activation(root[:, b], ss[:, b, 0:GW], ACT.Sqrt, bias=eps[:, 0:1]).then_inc(rooted, 1)
                    if to_sbuf:
                        act.wait_ge(scaled, i * 2 + b + 1)
                        nc.scalar.activation(xh[:, :, ds((i * 2 + b) * GW, GW)], x[:, b],
                                             ACT.Copy).then_inc(rounded, 1)
                    else:
                        act.wait_ge(stored, (i * 2 + b) * 16 + 16)
                        act.sem_inc(x_free, 1)

        @block.tensor
        def _(pe):
            pe.wait_ge(mean_set, 1)
            with pe.Fori(0, NG // 2) as i:
                for b in range(2):
                    pe.wait_ge(squared, i * 2 + b + 1)
                    for c in range(KC):
                        mm = pe.matmul(ss[:, b, 0:GW], mean[:], sq[:, b, c, :], start=(c == 0), stop=(c == KC - 1))
                    mm.then_inc(summed, 1)

        @block.vector
        def _(dve):
            dve.memset(eps[:], EPS).then_inc(eps_set, 1)
            dve.memset(mean[:], 1.0 / D).then_inc(mean_set, 1)
            if to_sbuf:
                dve.sem_inc(x_free, 2)
            dve.wait_ge(w_in, 16)
            with dve.Fori(0, NG // 2) as i:
                for b in range(2):
                    dve.wait_ge(rooted, i * 2 + b + 1)
                    dve.reciprocal(rstd[:, b], root[:, b])
                    dve.drain()
                    for c in range(KC):
                        ins = dve.scalar_tensor_tensor(x[:, b, c], x[:, b, c], w[:, c:c + 1], rstd[:, b],
                                                       ALU.mult, ALU.mult)
                    ins.then_inc(scaled, 1)
                    if to_sbuf:
                        dve.wait_ge(rounded, i * 2 + b + 1)
                        g = ds((i * 2 + b) * GW, GW)
                        dve.tensor_tensor(xl[:, :, g], x[:, b], xh[:, :, g].bitcast(F32),
                                          ALU.subtract).then_inc(x_free, 1)


def split(nc, name, src, xh, xl):
    with Stage(nc, name) as st:
        x = st.sb("x", [P, 2, T])
        x_in = [st.sem(f"x_in{b}") for b in range(2)]
        x_free, rounded = st.sem("x_free"), st.sem("rounded")
        block = st.block()

        @block.sync
        def _(sp):
            with sp.Fori(0, KC // 2) as i:
                for b in range(2):
                    sp.wait_ge(x_free, i * 2 + b + 1)
                    sp.dma_start(x[:, b], src[ds((i * 2 + b) * P, P), :]).then_inc(x_in[b], 16)

        @block.scalar
        def _(act):
            with act.Fori(0, KC // 2) as i:
                for b in range(2):
                    act.wait_ge(x_in[b], i * 16 + 16)
                    nc.scalar.activation(xh[:, ds((i * 2 + b), 1), :], x[:, b:b + 1], ACT.Copy).then_inc(rounded, 1)

        @block.vector
        def _(dve):
            dve.sem_inc(x_free, 2)
            with dve.Fori(0, KC // 2) as i:
                for b in range(2):
                    dve.wait_ge(rounded, i * 2 + b + 1)
                    c = ds(i * 2 + b, 1)
                    dve.tensor_tensor(xl[:, c, :], x[:, b:b + 1], xh[:, c, :].bitcast(F32),
                                      ALU.subtract).then_inc(x_free, 1)


class Weights:

    def __init__(self, st):
        self.raw = st.sb("w_raw", [P, 2, KC, P])
        self.hi = st.sb("w_hi", [P, 2, KC, P], F32R)
        self.lo = st.sb("w_lo", [P, 2, KC, P], F32R)
        self.loaded = [st.sem(f"w_loaded{b}") for b in range(2)]
        self.raw_free = st.sem("w_raw_free")
        self.split_free = st.sem("w_split_free")
        self.begun = st.sem("w_begun")
        self.ready = st.sem("w_ready")

    def load(self, sp, w_dram, n, i, b):
        sp.wait_ge(self.raw_free, n + 1)
        sp.dma_start(self.raw[:, b], w_dram[ds(n, 1)].rearrange("a p c m -> p (a c) m")).then_inc(self.loaded[b], 16)

    def split(self, pool, n, i, b):
        pool.wait_ge(self.loaded[b], i * 16 + 16)
        pool.wait_ge(self.split_free, n + 1)
        pool.sem_inc(self.begun, 1)
        pool.tensor_copy(self.hi[:, b], self.raw[:, b])
        pool.drain()
        pool.tensor_tensor(self.lo[:, b], self.raw[:, b], self.hi[:, b].bitcast(F32), ALU.subtract)
        pool.drain()
        pool.sem_inc(self.ready, 1)
        pool.sem_inc(self.raw_free, 1)

    def product(self, pe, out, b, xh, xl, m):
        g = slice(m * GW, (m + 1) * GW)
        for c in range(KC):
            pe.matmul(out, self.hi[:, b, c], xh[:, c, g], start=(c == 0), stop=False)
            pe.matmul(out, self.hi[:, b, c], xl[:, c, g], start=False, stop=False)
            mm = pe.matmul(out, self.lo[:, b, c], xh[:, c, g], start=False, stop=(c == KC - 1))
        return mm


def project(nc, name, w_dram, nblk, xh, xl, dst, residual=None, silu=False):
    with Stage(nc, name) as st:
        w = Weights(st)
        out = st.sb("out", [P, 2, T])
        res = st.sb("res", [P, 2, T]) if residual is not None else None
        acc = st.psum("acc", [P, NG, 512])
        product = st.sem("product")
        even_out, odd_out = st.sem("even_out"), st.sem("odd_out")
        stored = [st.sem(f"stored{b}") for b in range(2)]
        res_in = [st.sem(f"res_in{b}") for b in range(2)]
        block = st.block()
        npair, odd = nblk // 2, nblk % 2

        def blocks(eng, body):
            with eng.Fori(0, npair) as i:
                for b in range(2):
                    body(i * 2 + b, i, b)
            if odd:
                body(nblk - 1, npair, 0)

        @block.sync
        def _(sp):
            def body(n, i, b):
                w.load(sp, w_dram, n, i, b)
                if residual is not None:
                    sp.wait_ge(stored[b], i * 16 + 16)
                    sp.dma_start(res[:, b], residual[ds(n * P, P), :]).then_inc(res_in[b], 16)
            blocks(sp, body)

        @block.gpsimd
        def _(pool):
            pool.sem_inc(w.raw_free, 2)
            blocks(pool, lambda n, i, b: w.split(pool, n, i, b))

        @block.tensor
        def _(pe):
            pe.sem_inc(w.split_free, 2)

            def body(n, i, b):
                pe.wait_ge(w.ready, n + 1)
                for m in range(NG):
                    pe.wait_ge(odd_out if m % 2 else even_out, n * 3 + m // 2 + 1)
                    mm = w.product(pe, acc[:, m, 0:GW], b, xh, xl, m)
                    mm.then_inc(product, 1)
                pe.wait_ge(product, (n + 1) * NG)
                pe.sem_inc(w.split_free, 1)
            blocks(pe, body)

        def silu_of(dst_, src_):
            return nc.scalar.activation(dst_, src_, ACT.Silu)

        def copy_group(eng, copy, n, i, b, m, done):
            eng.wait_ge(product, n * NG + m + 1)
            if m < 2:
                eng.wait_ge(stored[b], i * 16 + 16)
            g = slice(m * GW, (m + 1) * GW)
            if residual is None:
                copy(out[:, b, g], acc[:, m, 0:GW]).then_inc(done, 1)
            else:
                if m < 2:
                    eng.wait_ge(res_in[b], i * 16 + 16)
                nc.vector.tensor_tensor(out[:, b, g], acc[:, m, 0:GW], res[:, b, g], ALU.add).then_inc(done, 1)

        @block.scalar
        def _(act):
            act.sem_inc(stored[0], 16)
            act.sem_inc(stored[1], 16)
            if residual is None:
                act.sem_inc(even_out, 3)
            if silu:
                act.sem_inc(odd_out, 3)

            def body(n, i, b):
                for m in range(NG):
                    if silu or (m % 2 == 0 and residual is None):
                        copy_group(act, silu_of if silu else nc.scalar.copy, n, i, b, m, odd_out if m % 2 else even_out)
                act.wait_ge(even_out, n * 3 + 6)
                act.wait_ge(odd_out, n * 3 + 6)
                act.dma_start(dst[ds(n * P, P), :], out[:, b]).then_inc(stored[b], 16)
            blocks(act, body)
            act.wait_ge(stored[0], 16 * (npair + odd + 1))
            act.wait_ge(stored[1], 16 * (npair + 1))

        @block.vector
        def _(dve):
            if silu:
                return
            dve.sem_inc(odd_out, 3)
            if residual is not None:
                dve.sem_inc(even_out, 3)

            def body(n, i, b):
                for m in range(NG):
                    if m % 2 or residual is not None:
                        copy_group(dve, nc.vector.tensor_copy, n, i, b, m, odd_out if m % 2 else even_out)
            blocks(dve, body)
GDN_TAPS, SC_TAPS = 4, 3


def prompt_and_samples(buf, taps):
    return buf[:, taps - 1:], buf[:, taps - 1 + SEQ:].rearrange("p (s t) -> p s t", s=NS)


def convolve(dve, y, x, xs, w, taps):
    ys = y[:, SEQ:].rearrange("p (s t) -> p s t", s=NS)
    for i in range(taps):
        for o, v in ((y[:, 0:SEQ], x[:, i:i + SEQ]), (ys, xs[:, :, i:i + TS])):
            if i == 0:
                ins = dve.tensor_scalar(o, v, w[:, 0:1], None, ALU.mult)
            else:
                ins = dve.scalar_tensor_tensor(o, v, w[:, i:i + 1], o, ALU.mult, ALU.add)
        if i < taps - 1:
            dve.drain()
    return ins


def project_gdn(nc, name, w_dram, par_dram, xh, xl, dst, tail_dram):
    H = GDN_TAPS - 1
    NPAR = NS * H + GDN_TAPS
    with Stage(nc, name) as st:
        w = Weights(st)
        x = st.sb("x", [P, H + T])
        xs = st.sb("xs", [P, NS, H + TS])
        y = st.sb("y", [P, 2, T])
        sq = st.sb("sq", [P, T])
        root = st.sb("root", [P, T])
        par = st.sb("par", [P, 2, NPAR])
        tail = st.sb("tail", [P, 2, H * (1 + NS)])
        ones, eps = st.sb("ones", [P, P]), st.sb("eps", [P, 1])
        acc = st.psum("acc", [P, NG, 512])
        ss = st.psum("ss", [P, 2, 512])
        const_set = st.sem("const_set")
        par_in = [st.sem(f"par_in{b}") for b in range(2)]
        product, copied = st.sem("product"), st.sem("copied")
        convolved = st.sem("convolved")
        activated = st.sem("activated")
        squared, summed, rooted = st.sem("squared"), st.sem("summed"), st.sem("rooted")
        normed = st.sem("normed")
        tail_out = st.sem("tail_out")
        par_free = st.sem("par_free")
        stored = [st.sem(f"stored{b}") for b in range(2)]
        tail_stored = [st.sem(f"tail_stored{b}") for b in range(2)]
        block = st.block()
        NH2 = GH // 2
        blocks = [(j, j % 3, j // 3) for j in range(6)]

        @block.sync
        def _(sp):
            with sp.Fori(0, NH2) as i:
                for j, part, head in blocks:
                    n, b, k = i * 6 + j, j % 2, i * 3 + j // 2
                    w.load(sp, w_dram, n, k, b)
                    sp.wait_ge(par_free, n + 1)
                    sp.dma_start(par[:, b], par_dram[ds(n * P, P), :]).then_inc(par_in[b], 16)

        @block.gpsimd
        def _(pool):
            pool.sem_inc(w.raw_free, 2)
            with pool.Fori(0, NH2) as i:
                for j, part, head in blocks:
                    w.split(pool, i * 6 + j, i * 3 + j // 2, j % 2)

        @block.tensor
        def _(pe):
            pe.sem_inc(w.split_free, 2)
            pe.wait_ge(const_set, 2)

            def sums(i, head, part):
                k = i * 4 + head * 2 + part
                pe.wait_ge(squared, k + 1)
                for m in range(NG):
                    pe.wait_ge(rooted, k * NG + m + 1)
                    pe.matmul(ss[:, m % 2, 0:GW], ones[:], sq[:, m * GW:(m + 1) * GW],
                              start=True, stop=True).then_inc(summed, 1)

            with pe.Fori(0, NH2) as i:
                for j, part, head in blocks:
                    n, b = i * 6 + j, j % 2
                    pe.wait_ge(w.ready, n + 1)
                    for m in range(NG):
                        pe.wait_ge(copied, n * NG + m + 1)
                        w.product(pe, acc[:, m, 0:GW], b, xh, xl, m).then_inc(product, 1)
                    pe.wait_ge(product, (n + 1) * NG)
                    pe.sem_inc(w.split_free, 1)
                    if part:
                        sums(i, head, part - 1)

        @block.scalar
        def _(act):
            act.sem_inc(copied, NG)
            act.sem_inc(rooted, 2)
            for b in range(2):
                act.sem_inc(stored[b], 16)
                act.sem_inc(tail_stored[b], 16)
            act.wait_ge(const_set, 2)

            def roots(i, head, part):
                k = i * 4 + head * 2 + part
                for m in range(NG):
                    act.wait_ge(summed, k * NG + m + 1)
                    if m == 0:
                        act.wait_ge(normed, k + 1)
                    nc.scalar.activation(root[:, m * GW:(m + 1) * GW], ss[:, m % 2, 0:GW], ACT.Sqrt,
                                         bias=eps[:, 0:1]).then_inc(rooted, 1)

            def store(i, j, n):
                act.dma_start(dst[ds(n * P, P), :], y[:, j % 2]).then_inc(stored[j % 2], 16)

            with act.Fori(0, NH2) as i:
                for j, part, head in blocks:
                    n, b, k = i * 6 + j, j % 2, i * 3 + j // 2
                    act.wait_ge(convolved, n + 1)
                    for m in range(NG):
                        act.wait_ge(product, n * NG + m + 1)
                        nc.scalar.copy(x[:, H + m * GW:H + (m + 1) * GW], acc[:, m, 0:GW]).then_inc(copied, 1)
                    act.wait_ge(tail_out, n + 1)
                    act.dma_start(tail_dram[ds(n * P, P), :], tail[:, b]).then_inc(tail_stored[b], 16)
                    act.wait_ge(convolved, n + 2)
                    nc.scalar.activation(y[:, b], y[:, b], ACT.Silu).then_inc(activated, 1)
                    act.wait_ge(activated, n + 1)
                    if part:
                        roots(i, head, part - 1)
                    if part == 2:
                        store(i, j, n)
                    else:
                        nc.scalar.activation(sq[:], y[:, b], ACT.Square).then_inc(squared, 1)
                    if part:
                        act.wait_ge(normed, i * 4 + head * 2 + part + 1)
                        store(i, j - 1, n - 1)
            for b in range(2):
                act.wait_ge(stored[b], 16 * (3 * GH // 2 + 1))
                act.wait_ge(tail_stored[b], 16 * (3 * GH // 2 + 1))

        @block.vector
        def _(dve):
            dve.memset(ones[:], 1.0).then_inc(const_set, 1)
            dve.memset(eps[:], EPS).then_inc(const_set, 1)
            dve.memset(x[:, 0:H], 0.0)
            dve.drain()
            dve.sem_inc(convolved, 1)
            dve.sem_inc(normed, 1)
            dve.sem_inc(par_free, 2)
            _, own = prompt_and_samples(x, GDN_TAPS)

            def scale(i, head, part, b):
                k = i * 4 + head * 2 + part
                for m in range(NG):
                    g = slice(m * GW, (m + 1) * GW)
                    dve.wait_ge(rooted, k * NG + m + 3)
                    dve.reciprocal(root[:, g], root[:, g])
                    dve.drain()
                    ins = dve.scalar_tensor_tensor(y[:, b, g], y[:, b, g], P ** -0.5 if part == 0 else 1.0,
                                                   root[:, g], ALU.mult, ALU.mult)
                ins.then_inc(normed, 1)

            with dve.Fori(0, NH2) as i:
                for j, part, head in blocks:
                    n, b, k = i * 6 + j, j % 2, i * 3 + j // 2
                    dve.wait_ge(par_in[b], k * 16 + 16)
                    dve.tensor_copy(xs[:, :, 0:H], par[:, b, 0:NS * H].rearrange("p (s t) -> p s t", s=NS))
                    dve.wait_ge(copied, n * NG + 2 * NG)
                    dve.tensor_copy(xs[:, :, H:], own)
                    dve.drain()
                    dve.wait_ge(tail_stored[b], k * 16 + 16)
                    dve.tensor_copy(tail[:, b, 0:H], x[:, SEQ:SEQ + H])
                    dve.tensor_copy(tail[:, b, H:].rearrange("p (s t) -> p s t", s=NS),
                                    xs[:, :, TS:]).then_inc(tail_out, 1)
                    dve.wait_ge(stored[b], k * 16 + 16)
                    convolve(dve, y[:, b], x, xs, par[:, b, NS * H:], GDN_TAPS).then_inc(convolved, 1)
                    if part:
                        scale(i, head, part - 1, 1 - b)
                    dve.drain()
                    dve.sem_inc(par_free, 1)


def shortconv(nc, name, w_dram, par_dram, xh, xl, dst, tail_dram):
    H = SC_TAPS - 1
    NPAR = NS * H + SC_TAPS
    with Stage(nc, name) as st:
        w = Weights(st)
        u, gb, gz, y = (st.sb(s, [P, T]) for s in ("u", "gb", "gz", "y"))
        x = st.sb("x", [P, H + T])
        xs = st.sb("xs", [P, NS, H + TS])
        par = st.sb("par", [P, NPAR])
        tail = st.sb("tail", [P, H * (1 + NS)])
        acc = st.psum("acc", [P, NG, 512])
        par_in = st.sem("par_in")
        product = st.sem("product")
        u_out, gb_out, gz_out = st.sem("u_out"), st.sem("gb_out"), st.sem("gz_out")
        cu_out = st.sem("cu_out")
        convolved, gated = st.sem("convolved"), st.sem("gated")
        tail_out = st.sem("tail_out")
        stored, tail_stored = st.sem("stored"), st.sem("tail_stored")
        block = st.block()
        NJ = D // P

        @block.sync
        def _(sp):
            with sp.Fori(0, NJ) as i:
                for part in range(4):
                    w.load(sp, w_dram, i * 4 + part, i * 2 + part // 2, part % 2)
                sp.wait_ge(tail_stored, i * 16 + 16)
                sp.wait_ge(stored, i * 16 + 16)
                sp.dma_start(par[:], par_dram[ds(i * P, P), :]).then_inc(par_in, 16)

        @block.gpsimd
        def _(pool):
            pool.sem_inc(w.raw_free, 2)
            with pool.Fori(0, NJ) as i:
                for part in range(4):
                    w.split(pool, i * 4 + part, i * 2 + part // 2, part % 2)

        @block.tensor
        def _(pe):
            pe.sem_inc(w.split_free, 2)
            with pe.Fori(0, NJ) as i:
                for part in range(4):
                    n = i * 4 + part
                    pe.wait_ge(w.ready, n + 1)
                    for m in range(NG):
                        before, start = [(gz_out, 0), (u_out, 0), (gb_out, 0), (cu_out, NG)][part]
                        pe.wait_ge(before, i * NG + start + m + 1)
                        w.product(pe, acc[:, m, 0:GW], part % 2, xh, xl, m).then_inc(product, 1)
                    pe.wait_ge(product, (n + 1) * NG)
                    pe.sem_inc(w.split_free, 1)

        def group(m):
            return slice(m * GW, (m + 1) * GW)

        @block.scalar
        def _(act):
            act.sem_inc(gz_out, NG)
            act.sem_inc(stored, 16)
            act.sem_inc(tail_stored, 16)
            with act.Fori(0, NJ) as i:
                act.wait_ge(cu_out, i * NG + NG)
                for m in range(NG):
                    act.wait_ge(product, i * 4 * NG + m + 1)
                    nc.scalar.copy(u[:, group(m)], acc[:, m, 0:GW]).then_inc(u_out, 1)
                act.wait_ge(gated, i * 1 + 1)
                for m in range(NG):
                    act.wait_ge(product, (i * 4 + 1) * NG + m + 1)
                    nc.scalar.copy(gb[:, group(m)], acc[:, m, 0:GW]).then_inc(gb_out, 1)
                for m in range(NG):
                    act.wait_ge(product, (i * 4 + 3) * NG + m + 1)
                    nc.scalar.activation(gz[:, group(m)], acc[:, m, 0:GW], ACT.Silu).then_inc(gz_out, 1)
                act.wait_ge(tail_out, i + 1)
                act.dma_start(tail_dram[ds(i * P, P), :], tail[:]).then_inc(tail_stored, 16)
                act.wait_ge(gated, i + 2)
                act.dma_start(dst[ds(i * P, P), :], y[:]).then_inc(stored, 16)
            act.wait_ge(stored, 16 * (NJ + 1))
            act.wait_ge(tail_stored, 16 * (NJ + 1))

        @block.vector
        def _(dve):
            dve.memset(x[:, 0:H], 0.0)
            dve.drain()
            dve.sem_inc(cu_out, NG)
            dve.sem_inc(gated, 1)
            _, own = prompt_and_samples(x, SC_TAPS)
            with dve.Fori(0, NJ) as i:
                for m in range(NG):
                    dve.wait_ge(u_out, i * NG + m + 1)
                    dve.wait_ge(product, (i * 4 + 2) * NG + m + 1)
                    dve.tensor_tensor(x[:, H + m * GW:H + (m + 1) * GW], acc[:, m, 0:GW], u[:, group(m)],
                                      ALU.mult).then_inc(cu_out, 1)
                dve.drain()
                dve.wait_ge(par_in, i * 16 + 16)
                dve.tensor_copy(xs[:, :, 0:H], par[:, 0:NS * H].rearrange("p (s t) -> p s t", s=NS))
                dve.tensor_copy(xs[:, :, H:], own)
                dve.drain()
                dve.tensor_copy(tail[:, 0:H], x[:, SEQ:SEQ + H])
                dve.tensor_copy(tail[:, H:].rearrange("p (s t) -> p s t", s=NS), xs[:, :, TS:]).then_inc(tail_out, 1)
                dve.wait_ge(stored, i * 16 + 16)
                convolve(dve, y, x, xs, par[:, NS * H:], SC_TAPS)
                dve.drain()
                dve.wait_ge(gb_out, i * NG + NG)
                dve.tensor_tensor(y[:], y[:], gb[:], ALU.mult)
                dve.drain()
                dve.wait_ge(gz_out, i * NG + 2 * NG)
                dve.tensor_tensor(y[:], y[:], gz[:], ALU.mult).then_inc(gated, 1)
                dve.drain()
def constants():
    k, q = np.arange(P)[:, None], np.arange(P)[None, :]
    own = (k // TS == q // TS) & (k < NS * TS) & (q < NS * TS)
    level = lambda s: (k // (2 * s) == q // (2 * s)) & (k // s != q // s) & (k > q)
    mats = dict(
        ident=k == q,
        suffix=-1.0 * (k >= q),
        earlier=k < q,
        not_earlier=-1e30 * (k >= q),
        upto=k <= q,
        later=-1e30 * (k > q),
        upto_own=(k <= q) & own,
        later_own=-1e30 * ~((k <= q) & own),
        diag16=(k // 16 == q // 16),
        level16=level(16), level32=level(32), level64=level(64),
    )
    assert list(mats) == CONST
    return np.stack([m.astype(np.float32) for m in mats.values()], 1)


CONST = ["ident", "suffix", "earlier", "not_earlier", "upto", "later", "upto_own", "later_own",
         "diag16", "level16", "level32", "level64"]


def const(dram, name):
    return dram[:, CONST.index(name)]


def softplus(nc, act, z, t):
    nc.scalar.activation(t, z, ACT.Abs)
    act.drain()
    nc.scalar.activation(t, t, ACT.Exp, scale=-1.0)
    act.drain()
    return nc.scalar.activation(t, t, ACT.Ln, bias=1.0)


def prompt_attention(nc, name, proj, bias_dram, const_dram, mix):
    DA = SBD + 1
    GQ = 512
    NKG = GQ // P
    NGQ = SEQ // GQ
    NB = SEQ // P
    head_steps = [(g, kb) for g in range(NGQ) for kb in range(NKG * (g + 1) - 1, -1, -1)]
    NSTEP = len(head_steps)
    steps = [(b, g, kb) for b in range(2) for g, kb in head_steps]
    N2 = len(steps)
    with Stage(nc, name) as st:
        q, k = st.sb("q", [DA, 2, SEQ]), st.sb("k", [DA, 2, SEQ])
        v, gate = st.sb("v", [SBD, 2, SEQ]), st.sb("gate", [SBD, 2, SEQ])
        vt = st.sb("vt", [P, 2, NB, SBD])
        bias = st.sb("bias", [DA, SBH])
        ident, suffix, earlier, masked, minus = (st.sb(s, [P, P]) for s in
                                                 ("ident", "suffix", "earlier", "masked", "minus"))
        t, sp, acc, a = (st.sb(s, [P, 2, GQ]) for s in ("t", "sp", "acc", "a"))
        o = st.sb("o", [SBD, 2, GQ])
        z = st.psum("z", [P, 4, 512])
        out = st.psum("out", [SBD, 2, 512])
        vps = st.psum("vps", [P, 2, 512])
        const_in, minus_set = st.sem("const_in"), st.sem("minus_set")
        loaded = [[st.sem(f"loaded_{s}{b}") for b in range(2)] for s in "qkvz"]
        head_read = [st.sem(f"head_read{b}") for b in range(2)]
        gate_read = [st.sem(f"gate_read{b}") for b in range(2)]
        summed = st.sem("summed")
        scaled = st.sem("scaled")
        turned = st.sem("turned")
        vt_out = st.sem("vt_out")
        scores = st.sem("scores")
        logs = st.sem("logs")
        plus = st.sem("plus")
        carried = st.sem("carried")
        weights = st.sem("weights")
        used = st.sem("used")
        gated = st.sem("gated")
        stored, o_free = st.sem("stored"), st.sem("o_free")
        turning = st.sem("turning")
        block = st.block()

        def columns(g, kb):
            c = max(0, kb - NKG * g) * P
            return c, kb >= NKG * g

        @block.sync
        def _(sp_):
            for dst, s in ((ident, "ident"), (suffix, "suffix"), (earlier, "earlier"), (masked, "not_earlier")):
                sp_.dma_start(dst[:], const(const_dram, s)).then_inc(const_in, 16)
            sp_.dma_start(bias[SBD:DA], bias_dram).then_inc(const_in, 16)
            with sp_.Fori(0, SBH // 2) as i:
                for b in range(2):
                    sp_.wait_ge(head_read[b], i + 1)
                    sp_.wait_ge(gate_read[b], i + 1)
                    for s, (dst, row) in enumerate(((q, Q0), (k, K0), (v, V0), (gate, Z0))):
                        sp_.dma_start(dst[0:SBD, b], proj[ds((i * 2 + b) * SBD + row * P, SBD), 0:SEQ]
                                      ).then_inc(loaded[s][b], 16)

        @block.gpsimd
        def _(pool):
            pool.sem_inc(o_free, 2)
            with pool.Fori(0, SBH // 2) as i:
                for b in range(2):
                    for g in range(NGQ):
                        n = i * 2 * NGQ + b * NGQ + g
                        pool.wait_ge(gated, n + 3)
                        pool.dma_start(mix[ds((i * 2 + b) * SBD, SBD), g * GQ:(g + 1) * GQ],
                                       o[:, g % 2]).then_inc(stored, 16)
                        pool.wait_ge(stored, n * 16 + 16)
                        pool.sem_inc(o_free, 1)

        @block.tensor
        def _(pe):
            pe.sem_inc(carried, 2)
            pe.sem_inc(used, 2)
            pe.sem_inc(head_read[0], 1)
            pe.sem_inc(head_read[1], 1)
            pe.wait_ge(const_in, 16 * 5)
            pe.wait_ge(minus_set, 1)

            def turn_v(i, b):
                pe.wait_ge(loaded[2][b], i * 16 + 16)
                pe.wait_ge(vt_out, i * 2 + b + 1)
                pe.sem_inc(turning, 1)
                for kb in range(NB):
                    mm = pe.transpose(vps[:, kb // 8, (kb % 8) * SBD:(kb % 8 + 1) * SBD],
                                      v[:, b, kb * P:(kb + 1) * P], ident[0:SBD, 0:SBD])
                mm.then_inc(turned, 1)

            def score(i, s):
                b, g, kb = steps[s]
                c, _ = columns(g, kb)
                if s % NSTEP == 0:
                    pe.wait_ge(scaled, i * 2 + b + 1)
                pe.wait_ge(weights, i * N2 + s + 1)
                pe.matmul(z[:, s % 4, c:GQ], k[:, b, kb * P:(kb + 1) * P], q[:, b, g * GQ + c:(g + 1) * GQ],
                          start=True, stop=True).then_inc(scores, 1)

            def carry(i, s):
                b, g, kb = steps[s]
                c, diagonal = columns(g, kb)
                c1 = c + P if diagonal else c
                pe.wait_ge(plus, i * N2 + s + 3)
                mm = pe.matmul(z[:, s % 4, c:GQ], suffix[:], sp[:, s % 2, c:GQ], start=False, stop=True,
                               skip_group_check=True)
                if diagonal:
                    mm = pe.matmul(z[:, s % 4, c:c + P], ident[:], masked[:], start=False, stop=True,
                                   skip_group_check=True)
                if c1 < GQ:
                    pe.wait_ge(summed, i * N2 + s)
                    mm = pe.matmul(z[:, s % 4, c1:GQ], minus[:], acc[:, (s - 1) % 2, c1:GQ], start=False,
                                   stop=True, skip_group_check=True)
                mm.then_inc(carried, 1)

            def apply(i, s):
                b, g, kb = steps[s]
                c, _ = columns(g, kb)
                if s % NSTEP == 0:
                    pe.wait_ge(vt_out, i * 2 + b + 2)
                if kb == NKG * (g + 1) - 1:
                    pe.wait_ge(gated, i * 2 * NGQ + b * NGQ + g + 1)
                pe.wait_ge(weights, i * N2 + s + 5)
                mm = pe.matmul(out[:, g % 2, c:GQ], vt[:, b, kb], a[:, s % 2, c:GQ],
                               start=(kb == NKG * (g + 1) - 1), stop=(kb == 0), skip_group_check=True)
                mm.then_inc(used, 1)
                if s % NSTEP == NSTEP - 1:
                    pe.wait_ge(used, i * N2 + s + 3)
                    pe.sem_inc(head_read[b], 1)

            with pe.Fori(0, SBH // 2) as i:
                turn_v(i, 0)
                for s in range(N2 + 2):
                    if s == NSTEP // 2:
                        turn_v(i, 1)
                    if s < N2:
                        score(i, s)
                    if 1 <= s <= N2:
                        carry(i, s - 1)
                    if s >= 2:
                        apply(i, s - 2)

        @block.scalar
        def _(act):
            nc.scalar.preload_act_table_set("natural_log_exp_and_others")
            act.sem_inc(weights, 4)

            with act.Fori(0, SBH // 2) as i:
                for s in range(N2 + 1):
                    if s < N2:
                        b, g, kb = steps[s]
                        c, _ = columns(g, kb)
                        act.wait_ge(scores, i * N2 + s + 1)
                        act.wait_ge(plus, i * N2 + s + 1)
                        softplus(nc, act, z[:, s % 4, c:GQ], t[:, s % 2, c:GQ]).then_inc(logs, 1)
                    if s >= 1:
                        r = s - 1
                        c, _ = columns(*steps[r][1:])
                        act.wait_ge(carried, i * N2 + r + 3)
                        act.wait_ge(used, i * N2 + r + 1)
                        nc.scalar.activation(a[:, r % 2, c:GQ], z[:, r % 4, c:GQ], ACT.Exp).then_inc(weights, 1)

        @block.vector
        def _(dve):
            dve.memset(minus[:], -1.0).then_inc(minus_set, 1)
            dve.memset(q[SBD:DA], 1.0)
            dve.sem_inc(plus, 2)
            dve.sem_inc(gated, 2)
            dve.sem_inc(vt_out, 1)
            dve.sem_inc(gate_read[0], 1)
            dve.sem_inc(gate_read[1], 1)
            dve.wait_ge(const_in, 16 * 5)
            dve.drain()

            def prepare(i, b):
                for s in (0, 1):
                    dve.wait_ge(loaded[s][b], i * 16 + 16)
                dve.tensor_scalar(q[0:SBD, b], q[0:SBD, b], SBD ** -0.5, None, ALU.mult)
                dve.tensor_scalar(k[SBD:DA, b], q[SBD:DA, b], bias[SBD:DA, ds(i * 2 + b, 1)], None,
                                  ALU.mult).then_inc(scaled, 1)
                dve.wait_ge(turned, i * 2 + b + 1)
                dve.wait_ge(head_read[b], i + 1)
                dve.tensor_copy(vt[:, b].rearrange("p (a n) d -> p a (n d)", a=2), vps[:]).then_inc(vt_out, 1)

            with dve.Fori(0, SBH // 2) as i:
                prepare(i, 0)
                for s in range(N2):
                    b, g, kb = steps[s]
                    c, diagonal = columns(g, kb)
                    if s == NSTEP // 2:
                        prepare(i, 1)
                    dve.wait_ge(logs, i * N2 + s + 1)
                    dve.wait_ge(carried, i * N2 + s + 1)
                    dve.scalar_tensor_tensor(sp[:, s % 2, c:GQ], z[:, s % 4, c:GQ], 0.0, t[:, s % 2, c:GQ],
                                             ALU.max, ALU.add)
                    dve.drain()
                    if diagonal:
                        dve.tensor_tensor(sp[:, s % 2, c:c + P], sp[:, s % 2, c:c + P], earlier[:], ALU.mult)
                        dve.drain()
                    dve.sem_inc(plus, 1)
                    dve.wait_ge(carried, i * N2 + s + 2)
                    c1 = c + P if diagonal else c
                    if diagonal:
                        dve.tensor_copy(acc[:, s % 2, c:c + P], sp[:, s % 2, c:c + P])
                    if c1 < GQ:
                        dve.tensor_tensor(acc[:, s % 2, c1:GQ], acc[:, (s - 1) % 2, c1:GQ], sp[:, s % 2, c1:GQ],
                                          ALU.add)
                    dve.drain()
                    dve.sem_inc(summed, 1)
                    for r in ([s - 2] if s >= 2 and steps[s - 2][2] == 0 else []) + (
                            [s] if s == N2 - 1 else []):
                        rb, rg, _ = steps[r]
                        dve.wait_ge(used, i * N2 + r + 3)
                        if rg == 0:
                            dve.wait_ge(loaded[3][rb], i * 16 + 16)
                        dve.wait_ge(o_free, i * 2 * NGQ + rb * NGQ + rg + 1)
                        dve.tensor_tensor(o[:, rg % 2], out[:, rg % 2], gate[:, rb, rg * GQ:(rg + 1) * GQ],
                                          ALU.mult).then_inc(gated, 1)
                        if rg == NGQ - 1:
                            dve.drain()
                            dve.sem_inc(gate_read[rb], 1)


def own_rows():
    return (np.arange(P)[:, None] // TS == np.arange(NS)[None]).astype(np.float32)
def head_constants():
    r = np.arange(SBH * TS)[:, None]
    return np.concatenate([r // TS == np.arange(SBH * SBD)[None] // SBD, r % TS == np.arange(TS)[None]],
                          1).astype(np.float32)


def sample_attention(nc, name, proj, bias_dram, pages_dram, k_pool, v_pool, const_dram, heads_dram, mix):
    NP = 8
    NB = NPAGE // NP
    NX = NS * NB
    HQ = SBH * TS
    NC = SBH // 2
    C2 = 2 * TS
    W = NP * HQ
    assert W == 512 and NS * HQ == 512
    with Stage(nc, name) as st:
        kp = st.sb("kp", [P, 2, NP, NC, PAGE])
        vp = st.sb("vp", [P, 2, NP, NC * P])
        table = st.sb("table", [1, NX * NP], I32)
        qn, kn, vn, zn = (st.sb(s, [P, NC, NS * TS]) for s in ("qn", "kn", "vn", "zn"))
        qb = st.sb("qb", [P, NS, NC, HQ])
        q_now = st.sb("q_now", [P, 2, NC, HQ])
        heads = st.sb("heads", [HQ, NC * P])
        pick = st.sb("pick", [HQ, TS])
        vt = st.sb("vt", [TS, NS, NC * P])
        bias = st.sb("bias", [1, SBH])
        bias_row = st.sb("bias_row", [1, NP, SBH, TS])
        ones_row = st.sb("ones_row", [1, P])
        ident, suffix, earlier, masked, minus = (st.sb(s, [P, P]) for s in
                                                 ("ident", "suffix", "earlier", "masked", "minus"))
        mask_new = st.sb("mask_new", [TS, W])
        t, sp, acc, a = (st.sb(s, [P, 2, W]) for s in ("t", "sp", "acc", "a"))
        carry_in = st.sb("carry_in", [P, NS * (NB + 1), HQ])
        total = st.sb("total", [HQ, NS, NC * P])
        o = st.sb("o", [P, NC, NS * TS])
        z = st.psum("z", [P, 2, 512])
        out = st.psum("out", [P, 2, 512])
        vps = st.psum("vps", [P, 4, 512])
        table_in, proj_in, const_in = st.sem("table_in"), st.sem("proj_in"), st.sem("const_in")
        k_in = [st.sem(f"k_in{b}") for b in range(2)]
        v_in = [st.sem(f"v_in{b}") for b in range(2)]
        k_read, v_read = st.sem("k_read"), st.sem("v_read")
        ready = st.sem("ready")
        turned, vt_out = st.sem("turned"), st.sem("vt_out")
        masked_out = st.sem("masked_out")
        new_scores, new_logs, new_plus, new_carried, new_weights, new_used, new_done = (
            st.sem(f"new_{s}") for s in ("scores", "logs", "plus", "carried", "weights", "used", "done"))
        scores, logs = st.sem("scores"), st.sem("logs")
        q_set = st.sem("q_set")
        plus, summed = st.sem("plus"), st.sem("summed")
        carried, weights, used, added = (st.sem(s) for s in ("carried", "weights", "used", "added"))
        stored = st.sem("stored")
        block = st.block()
        new = slice(SEQ, T)

        @block.sync
        def _(sp_):
            sp_.dma_start(table[:], pages_dram).then_inc(table_in, 16)
            for dst, row in ((qn, Q0), (kn, K0), (vn, V0), (zn, Z0)):
                sp_.dma_start(dst[:], proj[row * P:(row + NC) * P, new].rearrange("(c p) t -> p c t", p=P)
                              ).then_inc(proj_in, 16)
            for dst, s in ((ident, "ident"), (suffix, "suffix"), (earlier, "earlier"), (masked, "not_earlier")):
                sp_.dma_start(dst[:], const(const_dram, s)).then_inc(const_in, 16)
            sp_.dma_start(bias[:], bias_dram).then_inc(const_in, 16)
            sp_.dma_start(heads[:], heads_dram[:, 0:NC * P]).then_inc(const_in, 16)
            sp_.dma_start(pick[:], heads_dram[:, NC * P:]).then_inc(const_in, 16)
            sp_.wait_ge(table_in, 16)
            with sp_.Fori(0, NX // 2) as i:
                for b in range(2):
                    x = i * 2 + b
                    pages = [sp_.value_load(table[0:1, ds(x * NP + p, 1)], min_val=0,
                                            max_val=k_pool.shape[0] - 1) for p in range(NP)]
                    sp_.wait_ge(k_read, x + 1)
                    for p in range(NP):
                        sp_.dma_start(kp[:, b, p], k_pool[ds(pages[p], 1)].rearrange("a p c k -> p (a c) k")
                                      ).then_inc(k_in[b], 16)
                    sp_.wait_ge(v_read, x + 1)
                    for p in range(NP):
                        sp_.dma_start(vp[:, b, p], v_pool[ds(pages[p], 1)].rearrange("a k e -> k (a e)")
                                      ).then_inc(v_in[b], 16)
            sp_.wait_ge(new_done, 1)
            sp_.dma_start(mix[0:NC * P, new].rearrange("(c p) t -> p c t", p=P), o[:]).then_inc(stored, 16)
            sp_.wait_ge(stored, 16)

        @block.tensor
        def _(pe):
            pe.sem_inc(k_read, 2)
            pe.sem_inc(v_read, 2)
            pe.sem_inc(carried, 2)
            pe.sem_inc(used, 2)
            pe.wait_ge(const_in, 16 * 7)
            pe.wait_ge(proj_in, 16 * 4)
            for half in range(2):
                if half:
                    pe.wait_ge(vt_out, 1)
                for s in range(4):
                    for c in range(NC):
                        mm = pe.transpose(vps[0:TS, s, c * P:(c + 1) * P],
                                          vn[:, c, (half * 4 + s) * TS:(half * 4 + s + 1) * TS], ident[:])
                mm.then_inc(turned, 1)
            pe.wait_ge(ready, 1)
            pe.matmul(z[0:TS, 0], ones_row[:, 0:TS], bias_row[:].rearrange("a p h q -> a (p h q)"), start=True,
                      stop=False, skip_group_check=True)
            for s in range(NS):
                for c in range(NC):
                    col = s * HQ + c * C2
                    mm = pe.matmul(z[0:TS, 0, col:col + C2], kn[:, c, s * TS:(s + 1) * TS],
                                   qb[:, s, c, c * C2:(c + 1) * C2],
                                   start=False, stop=True, skip_group_check=True)
            mm.then_inc(new_scores, 1)
            pe.wait_ge(new_plus, 1)
            pe.matmul(z[0:TS, 0], suffix[0:TS, 0:TS], sp[0:TS, 0], start=False, stop=True, skip_group_check=True)
            pe.matmul(z[0:TS, 0], ident[0:TS, 0:TS], mask_new[:], start=False, stop=True,
                      skip_group_check=True).then_inc(new_carried, 1)
            pe.wait_ge(new_weights, 1)
            pe.wait_ge(vt_out, 2)
            for s in range(NS):
                pe.wait_ge(added, s + 1)
                pe.matmul(out[0:HQ, s % 2], a[0:TS, 0, s * HQ:(s + 1) * HQ], vt[:, s],
                          start=True, stop=True).then_inc(new_used, 1)

            def score(x, i, b):
                pe.wait_ge(k_in[b], (i + 1) * (16 * NP))
                pe.wait_ge(q_set, x + 1)
                pe.wait_ge(weights, x + 1)
                pe.matmul(z[:, b], ones_row[:], bias_row[:].rearrange("a p h q -> a (p h q)"), start=True,
                          stop=False, skip_group_check=True)
                for p in range(NP):
                    for c in range(NC):
                        mm = pe.matmul(z[:, b, p * HQ:(p + 1) * HQ], kp[:, b, p, c], q_now[:, b, c],
                                       start=False, stop=True, skip_group_check=True)
                mm.then_inc(scores, 1)
                pe.wait_ge(scores, x + 1)
                pe.sem_inc(k_read, 1)

            def rest(x, i, b):
                pe.wait_ge(plus, x + 3)
                pe.matmul(z[:, b], suffix[:], sp[:, b], start=False, stop=True, skip_group_check=True)
                pe.wait_ge(summed, x + 1)
                pe.matmul(z[:, b], minus[:], acc[:, b], start=False, stop=True,
                          skip_group_check=True).then_inc(carried, 1)
                pe.wait_ge(v_in[b], (i + 1) * (16 * NP))
                pe.wait_ge(added, NS + x + 1)
                pe.wait_ge(weights, x + 3)
                for p in range(NP):
                    mm = pe.matmul(out[0:HQ, b], a[:, b, p * HQ:(p + 1) * HQ], vp[:, b, p],
                                   start=(p == 0), stop=(p == NP - 1))
                mm.then_inc(used, 1)
                pe.wait_ge(used, x + 3)
                pe.sem_inc(v_read, 1)

            score(0, 0, 0)
            with pe.Fori(0, NX // 2 - 1) as i:
                score(i * 2 + 1, i, 1)
                rest(i * 2, i, 0)
                score(i * 2 + 2, i + 1, 0)
                rest(i * 2 + 1, i, 1)
            score(NX - 1, NX // 2 - 1, 1)
            rest(NX - 2, NX // 2 - 1, 0)
            rest(NX - 1, NX // 2 - 1, 1)
            pe.wait_ge(masked_out, 1)
            for c in range(NC):
                for s in range(NS):
                    col = (c * NS + s) * TS
                    mm = pe.matmul(vps[:, 0, col:col + TS], total[:, s, c * P:(c + 1) * P], pick[:],
                                   start=True, stop=True)
            mm.then_inc(turned, 1)

        @block.scalar
        def _(act):
            nc.scalar.preload_act_table_set("natural_log_exp_and_others")
            act.wait_ge(new_scores, 1)
            softplus(nc, act, z[0:TS, 0], t[0:TS, 0]).then_inc(new_logs, 1)
            act.wait_ge(new_carried, 1)
            nc.scalar.activation(a[0:TS, 0], z[0:TS, 0], ACT.Exp).then_inc(new_weights, 1)
            act.wait_ge(new_used, NS)
            act.wait_ge(new_weights, 1)
            act.sem_inc(weights, 2)

            def log(x, b):
                act.wait_ge(scores, x + 1)
                act.wait_ge(plus, x + 1)
                softplus(nc, act, z[:, b], t[:, b]).then_inc(logs, 1)

            def weigh(x, b):
                act.wait_ge(carried, x + 3)
                act.wait_ge(used, x + 1)
                nc.scalar.activation(a[:, b], z[:, b], ACT.Exp).then_inc(weights, 1)

            log(0, 0)
            with act.Fori(0, NX // 2 - 1) as i:
                weigh(i * 2, 0)
                log(i * 2 + 1, 1)
                weigh(i * 2 + 1, 1)
                log(i * 2 + 2, 0)
            weigh(NX - 2, 0)
            log(NX - 1, 1)
            weigh(NX - 1, 1)

        @block.vector
        def _(dve):
            dve.memset(minus[:], -1.0)
            dve.memset(ones_row[:], 1.0)
            dve.memset(qb[:], 0.0)
            dve.memset(carry_in[:], 0.0)
            dve.wait_ge(const_in, 16 * 7)
            dve.wait_ge(proj_in, 16 * 4)
            dve.drain()
            dve.tensor_copy(bias_row[:], bias[:].rearrange("a (p h q) -> a p h q", p=1, q=1)
                            .to_broadcast([1, NP, SBH, TS]))
            dve.tensor_copy(mask_new[:].rearrange("k (n q) -> k n q", q=TS),
                            masked[0:TS, 0:TS].rearrange("k (n q) -> k n q", n=1).to_broadcast([TS, W // TS, TS]))
            for s in range(NS):
                for hh in range(2):
                    r = slice(hh * SBD, (hh + 1) * SBD)
                    for c in range(NC):
                        h = c * 2 + hh
                        dve.tensor_scalar(qb[r, s, c, h * TS:(h + 1) * TS], qn[r, c, s * TS:(s + 1) * TS],
                                          SBD ** -0.5, None, ALU.mult)
            dve.drain()
            dve.sem_inc(ready, 1)
            for half in range(2):
                dve.wait_ge(turned, half + 1)
                dve.tensor_copy(vt[:, half * 4:half * 4 + 4], vps[0:TS]).then_inc(vt_out, 1)
            dve.wait_ge(new_logs, 1)
            dve.scalar_tensor_tensor(sp[0:TS, 0], z[0:TS, 0], 0.0, t[0:TS, 0], ALU.max, ALU.add)
            dve.drain()
            dve.tensor_tensor(sp[0:TS, 0].rearrange("k (n q) -> k n q", q=TS),
                              sp[0:TS, 0].rearrange("k (n q) -> k n q", q=TS),
                              earlier[0:TS, 0:TS].rearrange("k (n q) -> k n q", n=1).to_broadcast([TS, W // TS, TS]),
                              ALU.mult)
            dve.drain()
            dve.sem_inc(new_plus, 1)
            for s in range(NS):
                dve.tensor_copy(carry_in[0:TS, s * (NB + 1)], sp[0:TS, 0, s * HQ:(s + 1) * HQ])
            dve.sem_inc(added, 2)
            for s in range(NS):
                dve.wait_ge(new_used, s + 1)
                dve.tensor_copy(total[:, s], out[0:HQ, s % 2]).then_inc(added, 1)
            dve.drain()
            dve.sem_inc(plus, 2)

            def sum_later(x, b):
                dve.wait_ge(logs, x + 1)
                dve.wait_ge(carried, x + 1)
                dve.scalar_tensor_tensor(sp[:, b], z[:, b], 0.0, t[:, b], ALU.max, ALU.add).then_inc(plus, 1)
                dve.tensor_copy(acc[:, b, 0:HQ], carry_in[:, ds(x + x // NB, 1)].rearrange("p a c -> p (a c)"))
                dve.drain()
                for p in range(NP - 1):
                    ins = dve.tensor_tensor(acc[:, b, (p + 1) * HQ:(p + 2) * HQ], acc[:, b, p * HQ:(p + 1) * HQ],
                                            sp[:, b, p * HQ:(p + 1) * HQ], ALU.add)
                    if p < NP - 2:
                        dve.drain()
                ins.then_inc(summed, 1)
                dve.drain()
                dve.tensor_tensor(carry_in[:, ds(x + x // NB + 1, 1)].rearrange("p a c -> p (a c)"),
                                  acc[:, b, W - HQ:], sp[:, b, W - HQ:], ALU.add)
                dve.drain()

            def add(x, b):
                s = ds(x // NB, 1)
                dve.wait_ge(used, x + 3)
                dve.tensor_tensor(total[:, s], out[0:HQ, b:b + 1], total[:, s], ALU.add).then_inc(added, 1)
                dve.drain()

            def set_q(x, b):
                dve.wait_ge(scores, x - 1)
                dve.tensor_copy(q_now[:, b:b + 1], qb[:, ds(x // NB, 1)]).then_inc(q_set, 1)

            for b in range(2):
                dve.tensor_copy(q_now[:, b], qb[:, 0]).then_inc(q_set, 1)
            sum_later(0, 0)
            with dve.Fori(0, NX // 2 - 1) as i:
                set_q(i * 2 + 2, 0)
                sum_later(i * 2 + 1, 1)
                add(i * 2, 0)
                set_q(i * 2 + 3, 1)
                sum_later(i * 2 + 2, 0)
                add(i * 2 + 1, 1)
            sum_later(NX - 1, 1)
            add(NX - 2, 0)
            add(NX - 1, 1)
            for s in range(NS):
                dve.tensor_tensor(total[:, s], total[:, s], heads[:], ALU.mult)
            dve.drain()
            dve.sem_inc(masked_out, 1)
            dve.wait_ge(turned, 3)
            dve.tensor_tensor(o[:], vps[:, 0, 0:NC * NS * TS].rearrange("p (c t) -> p c t", c=NC), zn[:],
                              ALU.mult).then_inc(new_done, 1)
def gdn(nc, name, proj, qkv, rate_dram, out_w_dram, const_dram, own_dram, state_dram, mix, new_state, new_states):
    NCH = SEQ // P
    H = GH
    with Stage(nc, name) as st:
        mat = lambda s: st.sb(s, [P, 2, H, P])
        col = lambda s: st.sb(s, [P, 2, H])
        x = st.sb("x", [P, 2, 3 * H, P])
        gate = st.sb("gate", [P, 2, H, P])
        ba = st.sb("ba", [2 * H, T])
        rate = st.sb("rate", [P, 2 * H])
        out_w = st.sb("out_w", [P, 1])
        beta, g, tmp = (st.sb(s, [P, NCH + 2, H]) for s in ("beta", "g", "tmp"))
        g_now, beta_now, minus_beta, gc, egc, k_scale, kd_scale, ss, rstd = (
            col(s) for s in ("g_now", "beta_now", "minus_beta", "gc", "egc", "k_scale", "kd_scale", "ss", "rstd"))
        consts = {s: st.sb(s, [P, P]) for s in CONST if s not in ("suffix", "not_earlier")}
        own_row = st.sb("own_row", [P, NS])
        ones, eps = st.sb("ones", [P, P]), st.sb("eps", [P, 1])
        gu, eg, dec, kk, qk, n, nb, nbt, y, r, yt = (mat(s) for s in (
            "gu", "eg", "dec", "kk", "qk", "n", "nb", "nbt", "y", "r", "yt"))
        p2, p2t, p4, p4t, p8 = (mat(s) for s in ("p2", "p2t", "p4", "p4t", "p8"))
        joins = [mat(f"join{l}") for l in (16, 32, 64)]
        vb, kbg, kd, qg, wn, vnew, on, o = (mat(s) for s in ("vb", "kbg", "kd", "qg", "wn", "vnew", "on", "o"))
        state = st.sb("state", [P, H, P])
        states = st.sb("states", [P, NS, H, P])
        w_own, q_own = (st.sb(s, [P, H, NS * (P + TS)]) for s in ("w_own", "q_own"))
        kd_own = st.sb("kd_own", [P, H, NS, P])
        bank = [st.psum(f"bank{j}", [P, H, P]) for j in range(6)]
        small = st.psum("small", [P, 2, 512])
        x_in = [st.sem(f"x_in{b}") for b in range(2)]
        const_in, ba_in, state_in, const_set = (st.sem(s) for s in ("const_in", "ba_in", "state_in", "const_set"))
        ba_turned, ba_exp, o_free = st.sem("ba_turned"), st.sem("ba_exp"), st.sem("o_free")
        pool_begun = st.sem("pool_begun")
        x_read = st.sem("x_read")
        stored = st.sem("stored")
        states_stored = st.sem("states_stored")
        PE = ["rows", "scores", "turned", "n_turned", "square2", "square4", "square8", "y8",
              "join0", "grow0", "join1", "grow1", "join2", "grow2", "w", "v_new", "out", "o_turned"]
        DV = ["decay_log", "m", "n", "y1", "y2", "y4", "y8", "y16", "y32", "y64", "state", "o"]
        AC = ["eg", "decay", "keys", "p2", "p4", "p8", "r0", "r1", "r2", "w", "v_new", "on"]
        PO = ["gu", "joins"]
        pe_step, dve_step, act_step, pool_step = (st.sem(s) for s in ("pe_step", "dve_step", "act_step", "pool_step"))
        now_set, scales = st.sem("now_set"), st.sem("scales")

        def count(names, late):
            k = names.index(late) if late else len(names)

            def value(pair, width, b, s):
                j = names.index(s)
                at = j * width + b if j < k else k * width + b * (len(names) - k) + j - k
                return pair * (2 * len(names)) + at + 1
            return value
        at_pe, at_dve, at_act, at_pool = count(PE, "v_new"), count(DV, "state"), count(AC, "v_new"), count(PO, None)
        block = st.block()
        heads = range(H)
        OWN_BANKS = (0, 3, 4, 5)

        def four(m):
            return m[:].rearrange("p (h c) -> p h c", h=1).to_broadcast([P, H, P])

        def pairs(eng, body):
            with eng.Fori(0, NCH // 2) as i:
                body(i, (0, 1), False)
            body(NCH // 2, (0,), True)

        @block.sync
        def _(sp):
            for s in consts:
                sp.dma_start(consts[s][:], const(const_dram, s)).then_inc(const_in, 16)
            for dst, src in ((rate, rate_dram), (out_w, out_w_dram), (own_row, own_dram)):
                sp.dma_start(dst[:], src).then_inc(const_in, 16)
            sp.dma_start(ba[:], proj[BA0 * P:BA0 * P + 2 * H]).then_inc(ba_in, 16)
            for s in range(NS):
                sp.dma_start(states[:, s], state_dram[s].rearrange("h k v -> k h v")).then_inc(state_in, 16)

            def body(i, pair, own):
                for b in pair:
                    wide = NS * TS if own else P
                    cols = slice(SEQ, T) if own else ds((i * 2 + b) * P, P)
                    sp.wait_ge(x_read, i * 2 + b + 1)
                    sp.dma_start(x[:, b, :, 0:wide], qkv[:, cols].rearrange("(m p) t -> p m t", p=P)).then_inc(x_in[b], 16)
                    sp.dma_start(gate[:, b, :, 0:wide], proj[GZ0 * P:(GZ0 + H) * P, cols].rearrange(
                        "(m p) t -> p m t", p=P)).then_inc(x_in[b], 16)
            pairs(sp, body)

        @block.gpsimd
        def _(pool):
            pool.sem_inc(o_free, 2)
            pool.wait_ge(const_set, 1)
            pool.wait_ge(const_in, 16 * (len(consts) + 3))

            def body(i, pair, own):
                upto = consts["upto_own" if own else "upto"]
                pool.wait_ge(now_set, i + 1)
                for b in pair:
                    pool.tensor_tensor(gu[:, b], upto[:].rearrange("p (h c) -> p h c", h=1).to_broadcast([P, H, P]),
                                       g_now[:, b].rearrange("p (h c) -> p h c", c=1).to_broadcast([P, H, P]),
                                       ALU.mult).then_inc(pool_step, 1)
                for b in pair:
                    pool.wait_ge(dve_step, at_dve(i, len(pair), b, "n"))
                    for l, s in enumerate((16, 32, 64)):
                        ins = pool.tensor_tensor(joins[l][:, b], n[:, b], four(consts[f"level{s}"]), ALU.mult)
                    ins.then_inc(pool_step, 1)
                for b in pair:
                    wide = NS * TS if own else P
                    cols = slice(SEQ, T) if own else ds((i * 2 + b) * P, P)
                    pool.wait_ge(dve_step, at_dve(i, len(pair), b, "o"))
                    pool.dma_start(mix[SBH * SBD:, cols].rearrange("(m p) t -> p m t", p=P), o[:, b, :, 0:wide]
                                   ).then_inc(stored, 16)
                pool.wait_ge(stored, (i * 2 + len(pair)) * 16)
                pool.sem_inc(o_free, len(pair))
            pairs(pool, body)
            pool.dma_start(new_state.rearrange("h k v -> k h v"), state[:]).then_inc(states_stored, 16)
            for s in range(NS):
                pool.dma_start(new_states[s].rearrange("h k v -> k h v"), states[:, s]).then_inc(states_stored, 16)
            pool.wait_ge(states_stored, 16 * (NS + 1))

        @block.tensor
        def _(pe):
            ident = consts["ident"]
            pe.wait_ge(const_in, 16 * (len(consts) + 3))
            pe.wait_ge(ba_in, 16)
            pe.wait_ge(const_set, 1)
            for c in range(NCH + 1):
                wide = P if c < NCH else NS * TS
                mm = pe.transpose(small[0:wide, 0, c * 2 * H:(c + 1) * 2 * H], ba[:, c * P:c * P + wide],
                                  ident[0:2 * H, 0:2 * H])
            mm.then_inc(ba_turned, 1)

            def each(out, lhs, rhs):
                for h in heads:
                    mm = pe.matmul(out[:, h], lhs[:, h], rhs[:, h], start=True, stop=True)
                return mm

            def turn(out, src):
                for h in heads:
                    mm = pe.transpose(out[:, h], src[:, h], ident[:])
                return mm

            def body(i, pair, own):
                width = len(pair)
                dve = lambda b, s: pe.wait_ge(dve_step, at_dve(i, width, b, s))
                act = lambda b, s: pe.wait_ge(act_step, at_act(i, width, b, s))
                pool = lambda b, s: pe.wait_ge(pool_step, at_pool(i, width, b, s))
                A, B, C = ([bank[3 * b + j] for b in range(2)] for j in range(3))
                upto = consts["upto_own" if own else "upto"]
                pe.wait_ge(now_set, i + 1)
                for b in pair:
                    pool(b, "gu")
                    pe.matmul(A[b][:].rearrange("p h c -> p (h c)"), ones[:], gu[:, b].rearrange("p h c -> p (h c)"),
                              start=True, stop=True)
                    pe.matmul(small[:, b, 0:H], upto[:], g_now[:, b], start=True, stop=True
                              ).then_inc(pe_step, 1)
                for b in pair:
                    q, k = x[:, b, 0:3 * H:3], x[:, b, 1:3 * H:3]
                    pe.wait_ge(x_in[b], (i + 1) * 32)
                    each(B[b], k, k)
                    each(C[b], k, q).then_inc(pe_step, 1)
                for b in pair:
                    dve(b, "m")
                    turn(C[b], kk[:, b])
                    turn(A[b], x[:, b, 1:3 * H:3])
                    turn(B[b], x[:, b, 2:3 * H:3]).then_inc(pe_step, 1)
                for b in pair:
                    dve(b, "n")
                    turn(C[b], n[:, b]).then_inc(pe_step, 1)
                for b in pair:
                    act(b, "keys")
                    dve(b, "y1")
                    each(A[b], nbt[:, b], nb[:, b])
                    each(B[b], nb[:, b], nbt[:, b]).then_inc(pe_step, 1)
                for b in pair:
                    act(b, "p2")
                    each(C[b], p2[:, b], y[:, b])
                    each(A[b], p2t[:, b], p2[:, b])
                    each(B[b], p2[:, b], p2t[:, b]).then_inc(pe_step, 1)
                for b in pair:
                    act(b, "p4")
                    dve(b, "y2")
                    each(A[b], p4t[:, b], p4[:, b])
                    each(C[b], p4[:, b], y[:, b]).then_inc(pe_step, 1)
                for b in pair:
                    act(b, "p8")
                    dve(b, "y4")
                    each(C[b], p8[:, b], y[:, b]).then_inc(pe_step, 1)
                for l, ready in enumerate(("y8", "y16", "y32")):
                    for b in pair:
                        dve(b, ready)
                        if l == 0:
                            pool(b, "joins")
                        each(A[b], joins[l][:, b], y[:, b])
                        turn(B[b], y[:, b]).then_inc(pe_step, 1)
                    for b in pair:
                        act(b, f"r{l}")
                        each(C[b], yt[:, b], r[:, b]).then_inc(pe_step, 1)
                for b in pair:
                    dve(b, "y64")
                    each(A[b], kbg[:, b], y[:, b]).then_inc(pe_step, 1)
                for b in pair:
                    act(b, "w")
                    for h in heads:
                        pe.matmul(B[b][:, h], y[:, b, h], vb[:, b, h], start=True, stop=False)
                        if not own:
                            if b and h == 0:
                                dve(0, "state")
                            elif h == 0:
                                pe.wait_ge(now_set, i + 1)
                            mm = pe.matmul(B[b][:, h], wn[:, b, h], state[:, h], start=False, stop=True)
                        else:
                            for s in range(NS):
                                mm = pe.matmul(B[b][:, h], w_own[:, h, s * P:(s + 1) * P], states[:, s, h],
                                               start=False, stop=(s == NS - 1))
                    mm.then_inc(pe_step, 1)
                    act(b, "v_new")
                    for h in heads:
                        if not own:
                            pe.matmul(C[b][:, h], qg[:, b, h], state[:, h], start=True, stop=False)
                        else:
                            for s in range(NS):
                                pe.matmul(C[b][:, h], q_own[:, h, s * P:(s + 1) * P], states[:, s, h],
                                          start=(s == 0), stop=False)
                        pe.matmul(C[b][:, h], qk[:, b, h], vnew[:, b, h], start=False, stop=True)
                    if not own:
                        mm = each(A[b], kd[:, b], vnew[:, b])
                    else:
                        for s in range(4):
                            for h in heads:
                                mm = pe.matmul(bank[OWN_BANKS[s]][:, h], kd_own[:, h, s], vnew[:, b, h],
                                               start=True, stop=True)
                    mm.then_inc(pe_step, 1)
                    act(b, "on")
                    turn(B[b], on[:, b]).then_inc(pe_step, 1)
                if own:
                    dve(0, "state")
                    for s in range(4, NS):
                        for h in heads:
                            mm = pe.matmul(bank[OWN_BANKS[s - 4]][:, h], kd_own[:, h, s], vnew[:, 0, h],
                                           start=True, stop=True)
                    mm.then_inc(pe_step, 1)
            pairs(pe, body)

        @block.scalar
        def _(act):
            nc.scalar.preload_act_table_set("natural_log_exp_and_others")
            act.wait_ge(const_in, 16 * (len(consts) + 3))
            act.wait_ge(const_set, 1)
            act.wait_ge(ba_exp, 1)
            nc.scalar.activation(beta[:], beta[:], ACT.Exp, scale=-1.0)
            nc.scalar.activation(rate[:, 0:H], rate[:, 0:H], ACT.Exp)
            softplus(nc, act, g[:], tmp[:]).then_inc(ba_exp, 1)
            copy = nc.scalar.copy

            def body(i, pair, own):
                pe = lambda b, s: act.wait_ge(pe_step, at_pe(i, len(pair), b, s))
                dve = lambda b, s: act.wait_ge(dve_step, at_dve(i, len(pair), b, s))
                A, B, C = ([bank[3 * b + j] for b in range(2)] for j in range(3))
                for b in pair:
                    pe(b, "rows")
                    nc.scalar.activation(eg[:, b], A[b][:], ACT.Exp).then_inc(act_step, 1)
                for b in pair:
                    dve(b, "decay_log")
                    nc.scalar.activation(egc[:, b], gc[:, b], ACT.Exp)
                    nc.scalar.activation(dec[:, b], dec[:, b], ACT.Exp).then_inc(act_step, 1)
                for b in pair:
                    act.wait_ge(scales, i * 2 + b + 1)
                    pe(b, "turned")
                    for h in heads:
                        nc.scalar.activation(kbg[:, b, h], A[b][:, h], ACT.Copy, scale=k_scale[:, b, h:h + 1])
                        nc.scalar.activation(kd[:, b, h], A[b][:, h], ACT.Copy, scale=kd_scale[:, b, h:h + 1])
                        ins = nc.scalar.activation(vb[:, b, h], B[b][:, h], ACT.Copy, scale=beta_now[:, b, h:h + 1])
                    ins.then_inc(act_step, 1)
                for b in pair:
                    pe(b, "square2")
                    copy(p2[:, b], A[b][:])
                    copy(p2t[:, b], B[b][:]).then_inc(act_step, 1)
                for b in pair:
                    pe(b, "square4")
                    copy(p4[:, b], A[b][:])
                    copy(p4t[:, b], B[b][:]).then_inc(act_step, 1)
                for b in pair:
                    pe(b, "square8")
                    copy(p8[:, b], A[b][:]).then_inc(act_step, 1)
                for l in range(3):
                    for b in pair:
                        pe(b, f"join{l}")
                        copy(r[:, b], A[b][:])
                        copy(yt[:, b], B[b][:]).then_inc(act_step, 1)
                for b in pair:
                    pe(b, "w")
                    if not own:
                        nc.scalar.mul(wn[:, b], A[b][:], -1.0).then_inc(act_step, 1)
                    else:
                        for h in heads:
                            mm = nc.scalar.mul(w_own[:, h].rearrange("p (s t) -> p s t", s=NS)[:, :, 0:TS],
                                               A[b][:, h, 0:NS * TS].rearrange("p (s t) -> p s t", s=NS), -1.0)
                        mm.then_inc(act_step, 1)
                for b in pair:
                    pe(b, "v_new")
                    copy(vnew[:, b], B[b][:]).then_inc(act_step, 1)
                    pe(b, "out")
                    for h in heads:
                        nc.scalar.activation(on[:, b, h], C[b][:, h], ACT.Square, accum_out=ss[:, b, h:h + 1])
                    act.drain()
                    nc.scalar.activation(ss[:, b], ss[:, b], ACT.Ln, scale=1.0 / P, bias=eps[:, 0:1])
                    act.drain()
                    nc.scalar.activation(rstd[:, b], ss[:, b], ACT.Exp, scale=-0.5)
                    act.drain()
                    for h in heads:
                        ins = nc.scalar.activation(on[:, b, h], C[b][:, h], ACT.Copy, scale=rstd[:, b, h:h + 1])
                    ins.then_inc(act_step, 1)
            pairs(act, body)

        @block.vector
        def _(dve):
            dve.memset(ones[:], 1.0)
            dve.memset(eps[:], EPS)
            for s in (beta, g, tmp, state, w_own, q_own, ss, x, gate):
                dve.memset(s[:], 0.0)
            dve.drain()
            dve.sem_inc(const_set, 1)
            dve.sem_inc(x_read, 2)
            dve.wait_ge(const_in, 16 * (len(consts) + 3))
            dve.wait_ge(state_in, 16 * NS)
            dve.wait_ge(ba_turned, 1)
            turned = small[:, 0, 0:(NCH + 1) * 2 * H].rearrange("p (c a h) -> p c a h", a=2, h=H)
            full, part = (slice(0, P), slice(0, NCH)), (slice(0, NS * TS), slice(NCH, NCH + 1))
            for rows, cs in (full, part):
                dve.tensor_copy(beta[rows, cs], turned[rows, cs, 0])
                dt = rate[rows, H:].rearrange("p (c h) -> p c h", c=1).to_broadcast([rows.stop, cs.stop - cs.start, H])
                dve.tensor_tensor(g[rows, cs], turned[rows, cs, 1], dt, ALU.add)
            dve.drain()
            dve.sem_inc(ba_exp, 1)
            dve.wait_ge(ba_exp, 2)
            dve.tensor_scalar(beta[:], beta[:], 1.0, None, ALU.add)
            dve.scalar_tensor_tensor(g[:], g[:], 0.0, tmp[:], ALU.max, ALU.add)
            dve.drain()
            dve.reciprocal(beta[:], beta[:])
            a = rate[:, 0:H].rearrange("p (c h) -> p c h", c=1).to_broadcast([P, NCH + 2, H])
            dve.scalar_tensor_tensor(g[:], g[:], -1.0, a, ALU.mult, ALU.mult)
            dve.drain()
            dve.memset(beta[NS * TS:, NCH], 0.0)
            dve.memset(g[NS * TS:, NCH], 0.0)
            dve.drain()

            def body(i, pair, own):
                pe = lambda b, s: dve.wait_ge(pe_step, at_pe(i, len(pair), b, s))
                act = lambda b, s: dve.wait_ge(act_step, at_act(i, len(pair), b, s))
                A, B, C = ([bank[3 * b + j] for b in range(2)] for j in range(3))
                later = consts["later_own" if own else "later"]
                tt, ts = dve.tensor_tensor, dve.tensor_scalar
                dve.tensor_copy(g_now[:], g[:, ds(i * 2, 2)])
                dve.tensor_copy(beta_now[:], beta[:, ds(i * 2, 2)])
                ts(minus_beta[:], beta[:, ds(i * 2, 2)], -1.0, None, ALU.mult)
                dve.drain()
                dve.sem_inc(now_set, 1)
                for b in pair:
                    act(b, "eg")
                    dve.tensor_copy(gc[:, b], small[:, b, 0:H])
                    dve.drain()
                    for h in heads:
                        ins = dve.scalar_tensor_tensor(dec[:, b, h], A[b][:, h], gc[:, b, h:h + 1], later[:],
                                                       ALU.subtract, ALU.add)
                    ins.then_inc(dve_step, 1)
                for b in pair:
                    act(b, "decay")
                    pe(b, "scores")
                    tt(kk[:, b], B[b][:], dec[:, b], ALU.mult)
                    tt(qk[:, b], C[b][:], dec[:, b], ALU.mult)
                    dve.drain()
                    tt(kk[:, b], kk[:, b], four(consts["earlier"]), ALU.mult).then_inc(dve_step, 1)
                    tt(k_scale[:, b], beta_now[:, b], egc[:, b], ALU.mult)
                    tt(qg[:, b], x[:, b, 0:3 * H:3], eg[:, b], ALU.mult)
                    if not own:
                        dve.tensor_copy(kd_scale[:, b], dec[:, b, :, P - 1])
                    else:
                        dve.tensor_reduce(kd_scale[:, b], dec[:, b, :, TS - 1:NS * TS:TS], mybir.AxisListType.X,
                                          ALU.add)
                    dve.drain()
                    dve.sem_inc(scales, 1)
                    if own:
                        for h in heads:
                            dve.tensor_copy(q_own[:, h].rearrange("p (s t) -> p s t", s=NS)[:, :, 0:TS],
                                            qg[:, b, h, 0:NS * TS].rearrange("p (s t) -> p s t", s=NS))
                for b in pair:
                    pe(b, "turned")
                    tt(n[:, b], C[b][:], minus_beta[:, b].rearrange("p (h c) -> p h c", c=1).to_broadcast([P, H, P]),
                       ALU.mult).then_inc(dve_step, 1)
                    dve.drain()
                    tt(nb[:, b], n[:, b], four(consts["diag16"]), ALU.mult)
                for b in pair:
                    pe(b, "n_turned")
                    tt(nbt[:, b], C[b][:], four(consts["diag16"]), ALU.mult)
                    dve.drain()
                    tt(y[:, b], nbt[:, b], four(consts["ident"]), ALU.add).then_inc(dve_step, 1)
                    dve.drain()
                if own:
                    act(0, "keys")
                    for h in heads:
                        for s in range(NS):
                            ts(kd_own[:, h, s], kd[:, 0, h], own_row[:, s:s + 1], None, ALU.mult)
                for product in ("square4", "square8", "y8", "grow0", "grow1", "grow2"):
                    for b in pair:
                        pe(b, product)
                        tt(y[:, b], C[b][:], y[:, b], ALU.add).then_inc(dve_step, 1)
                        dve.drain()

                def grow_states(samples):
                    for s in samples:
                        for h in heads:
                            last = s * TS + TS - 1
                            dve.scalar_tensor_tensor(states[:, s, h], states[:, s, h], eg[:, 0, h, last:last + 1],
                                                     bank[OWN_BANKS[s % 4]][:, h], ALU.mult, ALU.add)
                for b in pair:
                    pe(b, "out")
                    if not own:
                        for h in heads:
                            dve.scalar_tensor_tensor(state[:, h], state[:, h], eg[:, b, h, P - 1:P], A[b][:, h],
                                                     ALU.mult, ALU.add)
                    else:
                        grow_states(range(4))
                    dve.drain()
                    dve.sem_inc(dve_step, 1)
                    pe(b, "o_turned")
                    if own:
                        dve.wait_ge(pe_step, at_pe(i, 1, 0, "o_turned") + 1)
                        grow_states(range(4, NS))
                    dve.wait_ge(o_free, i * 2 + b + 1)
                    dve.scalar_tensor_tensor(o[:, b], B[b][:], out_w[:, 0:1], gate[:, b], ALU.mult, ALU.mult)
                    dve.drain()
                    dve.sem_inc(dve_step, 1)
                    dve.sem_inc(x_read, 1)
            pairs(dve, body)
def hybrid_step(nc, i, o, scratch):
    with nc.sbuf_tensor("xh", [P, KC, T], F32R) as xh, nc.sbuf_tensor("xl", [P, KC, T], F32R) as xl:
        norm(nc, "norm0", i["x"], i["norm_w0"], xh, xl, None)
        project(nc, "proj", i["w_in"], Z0, xh, xl, o["proj"][0:Z0 * P])
        project(nc, "gates", i["w_gates"], NROW - Z0, xh, xl, o["proj"][Z0 * P:], silu=True)
        project_gdn(nc, "projg", i["w_gdn"], i["par_gdn"], xh, xl, scratch["qkv"], o["tail_gdn"])
    prompt_attention(nc, "pattn", o["proj"], i["sb_bias"], i["const"], scratch["mix"])
    sample_attention(nc, "sattn", o["proj"], i["sb_bias"], i["pages"], i["k_pool"], i["v_pool"], i["const"],
                     i["head_const"], scratch["mix"])
    gdn(nc, "gdn", o["proj"], scratch["qkv"], i["rate"], i["out_norm_w"], i["const"], i["own_rows"], i["state"],
        scratch["mix"], o["new_state"], o["new_states"])
    with nc.sbuf_tensor("yh", [P, KC, T], F32R) as xh, nc.sbuf_tensor("yl", [P, KC, T], F32R) as xl:
        split(nc, "split0", scratch["mix"], xh, xl)
        project(nc, "out0", i["w_out0"], KC, xh, xl, scratch["h1"], residual=i["x"])
        norm(nc, "norm1", scratch["h1"], i["norm_w1"], xh, xl, None)
        shortconv(nc, "sconv", i["w_sc"], i["par_sc"], xh, xl, scratch["mix"], o["tail_sc"])
        split(nc, "split1", scratch["mix"], xh, xl)
        project(nc, "out1", i["w_out1"], KC, xh, xl, scratch["h2"], residual=scratch["h1"])
    norm(nc, "norm2", scratch["h2"], i["norm_w2"], None, None, o["y"])


def _blocks(w, order=None):
    w = np.pad(w, ((0, 0), (0, -w.shape[1] % P)))
    w = w.reshape(KC, P, -1, P).transpose(2, 1, 0, 3)
    return np.ascontiguousarray(w if order is None else w[order])


def _params(past, taps):
    n, t, c = past.shape
    return np.ascontiguousarray(np.concatenate([past.transpose(2, 0, 1).reshape(c, n * t), taps.T], 1))


GDN_ORDER = [part * GH + h for h in range(GH) for part in range(3)]
SC_ORDER = [part * KC + j for j in range(KC) for part in range(4)]


def kernel(x_prompt, x_sample, cache_sb_k, cache_sb_v, state_gdn, state_gdn_conv, state_sconv, page_table,
           norm_w, ab_w_in, ab_sb_bias, ab_conv_w, ab_a_log, ab_dt_bias, ab_out_norm_w, ab_w_out,
           sc_w_in, sc_conv_w, sc_w_out, final_norm_w):
    import concourse.bacc as _bacc
    from concourse.bass_utils import run_bass_kernel_spmd as _run

    a = np.asarray
    npool = cache_sb_k.shape[1]
    w_in = a(ab_w_in)[0]
    sbw, gw = 4 * SBH * SBD, 3 * GH * P
    col = lambda w: np.ascontiguousarray(a(w).reshape(KC, P).T)
    arrays = {
        "x": np.ascontiguousarray(np.concatenate([a(x_prompt).reshape(SEQ, D), a(x_sample).reshape(NS * TS, D)]).T),
        "norm_w0": col(norm_w[0]), "norm_w1": col(norm_w[1]), "norm_w2": col(final_norm_w),
        "w_in": _blocks(np.concatenate([w_in[:, :3 * SBH * SBD], w_in[:, sbw + gw + GH * P:]], 1)),
        "w_gates": _blocks(np.concatenate([w_in[:, 3 * SBH * SBD:sbw], w_in[:, sbw + gw:sbw + gw + GH * P]], 1)),
        "w_gdn": _blocks(w_in[:, sbw:sbw + gw], GDN_ORDER),
        "par_gdn": np.ascontiguousarray(
            _params(a(state_gdn_conv)[0], a(ab_conv_w)[0]).reshape(3 * GH, P, -1)[GDN_ORDER].reshape(gw, -1)),
        "sb_bias": a(ab_sb_bias),
        "const": constants(), "head_const": head_constants(), "own_rows": own_rows(),
        "pages": np.ascontiguousarray(a(page_table)[:, ::-1]).reshape(1, -1),
        "k_pool": np.ascontiguousarray(a(cache_sb_k)[0].reshape(npool, PAGE, SBH // 2, 2, SBD).transpose(0, 3, 4, 2, 1)
                                       ).reshape(npool, P, SBH // 2, PAGE),
        "v_pool": a(cache_sb_v)[0].reshape(npool, PAGE, SBH * SBD),
        "rate": np.repeat(np.concatenate([a(ab_a_log), a(ab_dt_bias)], 1), P, 0),
        "out_norm_w": np.ascontiguousarray(a(ab_out_norm_w).T),
        "state": a(state_gdn)[0],
        "w_out0": _blocks(a(ab_w_out)[0]),
        "w_sc": _blocks(a(sc_w_in)[0], SC_ORDER),
        "par_sc": _params(a(state_sconv)[0], a(sc_conv_w)[0]),
        "w_out1": _blocks(a(sc_w_out)[0]),
    }
    outs = {"proj": (NROW * P, T), "tail_gdn": (gw, 3 * (1 + NS)), "tail_sc": (D, 2 * (1 + NS)), "y": (D, T),
            "new_state": (GH, P, P), "new_states": (NS, GH, P, P)}
    temps = {"qkv": (gw, T), "mix": (D, T), "h1": (D, T), "h2": (D, T)}

    nc = _bacc.Bacc("TRN2", target_bir_lowering=False, num_devices=1)
    dram = lambda n, s, dt, kind: nc.dram_tensor(n, s, dt, kind=kind).ap()
    i = {n: dram(f"in_{n}", v.shape, mybir.dt.from_np(v.dtype), "ExternalInput") for n, v in arrays.items()}
    o = {n: dram(f"out_{n}", s, F32, "ExternalOutput") for n, s in outs.items()}
    scratch = {n: dram(f"tmp_{n}", s, F32, "Internal") for n, s in temps.items()}
    hybrid_step(nc, i, o, scratch)
    r = _run(nc, [{f"in_{n}": v for n, v in arrays.items()}], core_ids=[0]).results[0]
    r = {n: r[f"out_{n}"] for n in outs}

    def rows(m, prompt):
        return m[:, :SEQ].T[None] if prompt else m[:, SEQ:].T.reshape(NS, TS, -1)

    kv = [[rows(r["proj"][b * P:(b + 4) * P], p) for b in (K0, V0)] for p in (True, False)]
    kv = [[m.reshape(1, *m.shape[:2], SBH, SBD) for m in pair] for pair in kv]

    def tails(m, width):
        return m[:, :width].T[None, None], m[:, width:].reshape(-1, NS, width).transpose(1, 2, 0)[None]

    back = np.argsort(GDN_ORDER)
    gp, gs = tails(r["tail_gdn"].reshape(3 * GH, P, -1)[back].reshape(gw, -1), 3)
    sp, ss = tails(r["tail_sc"], 2)
    c = np.ascontiguousarray
    return (c(rows(r["y"], True)), c(rows(r["y"], False)), c(kv[0][0]), c(kv[0][1]), c(kv[1][0]), c(kv[1][1]),
            r["new_state"][None, None], r["new_states"][None], c(gp), c(gs), c(sp), c(ss))
```

```python
from contextlib import ExitStack

import numpy as np

import concourse.bass as bass
from concourse import mybir

F32 = mybir.dt.float32
F32R = mybir.dt.float32r
I32 = mybir.dt.int32
ACT = mybir.ActivationFunctionType
ALU = mybir.AluOpType
ds = bass.ds

P = 128
D = 1024
KC = D // P
SEQ = 2048
NS, TS = 8, 8
T = SEQ + NS * TS
NG = 6
GW = T // NG
assert GW * NG == T and GW <= 512
EPS = 1e-6
SBH, SBD = 8, 64
GH = 4
PAGE = 128
NPAGE = 64
Q0, K0, V0, BA0, Z0, GZ0, NROW = 0, 4, 8, 12, 13, 17, 21


class Stage:

    def __init__(self, nc, name):
        self.nc, self.name, self.ctx, self.sems = nc, name, ExitStack(), []

    def __enter__(self):
        return self

    def __exit__(self, *a):
        self.ctx.__exit__(*a)
        self.nc.clear_and_free_semaphores(self.sems)
        self.nc.all_engine_barrier()

    def sb(self, name, shape, dt=F32):
        return self.ctx.enter_context(self.nc.sbuf_tensor(f"{self.name}_{name}", shape, dt))

    def psum(self, name, shape):
        return self.ctx.enter_context(self.nc.psum_tensor(f"{self.name}_{name}", shape, F32))

    def sem(self, name):
        self.sems.append(self.nc.alloc_semaphore(f"{self.name}_{name}"))
        return self.sems[-1]

    def block(self):
        return self.ctx.enter_context(self.nc.Block())


def norm(nc, name, src, w_dram, xh, xl, dst):
    NX = 3
    with Stage(nc, name) as st:
        x = st.sb("x", [P, NX, KC, GW])
        sq = st.sb("sq", [P, 2, KC, GW])
        rstd = st.sb("rstd", [P, 2, GW])
        w = st.sb("w", [P, KC])
        mean = st.sb("mean", [P, P])
        eps = st.sb("eps", [P, 1])
        ss = st.psum("ss", [P, 2, 512])
        w_in, mean_set, eps_set = st.sem("w_in"), st.sem("mean_set"), st.sem("eps_set")
        x_in = [st.sem(f"x_in{b}") for b in range(NX)]
        squared, summed, rstd_set, scaled = (st.sem(s) for s in ("squared", "summed", "rstd_set", "scaled"))
        rounded, split_off = st.sem("rounded"), st.sem("split_off")
        stored = [st.sem(f"stored{b}") for b in range(NX)]
        block = st.block()
        to_sbuf = dst is None
        by_chunk = lambda m: m.rearrange("(c p) t -> p c t", p=P)
        group = lambda n: slice(n * GW, (n + 1) * GW)

        @block.sync
        def _(sp):
            sp.dma_start(w[:], w_dram).then_inc(w_in, 16)
            for n in range(NG):
                if n >= NX and to_sbuf:
                    sp.wait_ge(split_off, n - NX + 1)
                elif n >= NX:
                    sp.wait_ge(stored[n % NX], n // NX * 16)
                sp.dma_start(x[:, n % NX], by_chunk(src)[:, :, group(n)]).then_inc(x_in[n % NX], 16)

        @block.gpsimd
        def _(pool):
            if not to_sbuf:
                for n in range(NG):
                    pool.wait_ge(scaled, n + 1)
                    pool.dma_start(by_chunk(dst)[:, :, group(n)], x[:, n % NX]).then_inc(stored[n % NX], 16)
                for b in range(NX):
                    pool.wait_ge(stored[b], NG // NX * 16)

        @block.scalar
        def _(act):
            nc.scalar.preload_act_table_set("natural_log_exp_and_others")
            act.wait_ge(eps_set, 1)
            for s in range(NG + 2):
                if s < NG:
                    act.wait_ge(x_in[s % NX], s // NX * 16 + 16)
                    if s >= 2:
                        act.wait_ge(summed, s - 1)
                    nc.scalar.activation(sq[:, s % 2], x[:, s % NX], ACT.Square).then_inc(squared, 1)
                if 1 <= s <= NG:
                    n = s - 1
                    act.wait_ge(summed, n + 1)
                    if n >= 2:
                        act.wait_ge(scaled, n - 1)
                    nc.scalar.activation(rstd[:, n % 2], ss[:, n % 2, 0:GW], ACT.Ln, bias=eps[:, 0:1])
                    act.drain()
                    nc.scalar.activation(rstd[:, n % 2], rstd[:, n % 2], ACT.Exp, scale=-0.5).then_inc(rstd_set, 1)
                if s >= 2 and to_sbuf:
                    n = s - 2
                    act.wait_ge(scaled, n + 1)
                    nc.scalar.copy(xh[:, :, group(n)], x[:, n % NX]).then_inc(rounded, 1)

        @block.tensor
        def _(pe):
            pe.wait_ge(mean_set, 1)
            for n in range(NG):
                pe.wait_ge(squared, n + 1)
                if n >= 2:
                    pe.wait_ge(rstd_set, n - 1)
                for c in range(KC):
                    mm = pe.matmul(ss[:, n % 2, 0:GW], mean[:], sq[:, n % 2, c, :], start=(c == 0), stop=(c == KC - 1))
                mm.then_inc(summed, 1)

        @block.vector
        def _(dve):
            dve.memset(eps[:], EPS).then_inc(eps_set, 1)
            dve.memset(mean[:], 1.0 / D).then_inc(mean_set, 1)
            dve.wait_ge(w_in, 16)
            for s in range(NG + 1):
                if s < NG:
                    dve.wait_ge(rstd_set, s + 1)
                    for c in range(KC):
                        ins = dve.scalar_tensor_tensor(x[:, s % NX, c], x[:, s % NX, c], w[:, c:c + 1], rstd[:, s % 2],
                                                       ALU.mult, ALU.mult)
                    ins.then_inc(scaled, 1)
                if s >= 1 and to_sbuf:
                    n = s - 1
                    dve.wait_ge(rounded, n + 1)
                    dve.tensor_tensor(xl[:, :, group(n)], x[:, n % NX], xh[:, :, group(n)].bitcast(F32),
                                      ALU.subtract).then_inc(split_off, 1)


def split(nc, name, src, xh, xl):
    NX = 4
    with Stage(nc, name) as st:
        x = st.sb("x", [P, NX, T])
        x_in = [st.sem(f"x_in{b}") for b in range(NX)]
        x_free, rounded = st.sem("x_free"), st.sem("rounded")
        block = st.block()

        @block.sync
        def _(sp):
            with sp.Fori(0, KC // NX) as i:
                for b in range(NX):
                    sp.wait_ge(x_free, i * NX + b + 1)
                    sp.dma_start(x[:, b], src[ds((i * NX + b) * P, P), :]).then_inc(x_in[b], 16)

        @block.scalar
        def _(act):
            with act.Fori(0, KC // NX) as i:
                for b in range(NX):
                    act.wait_ge(x_in[b], i * 16 + 16)
                    nc.scalar.activation(xh[:, ds((i * NX + b), 1), :], x[:, b:b + 1], ACT.Copy).then_inc(rounded, 1)

        @block.vector
        def _(dve):
            dve.sem_inc(x_free, NX)
            with dve.Fori(0, KC // NX) as i:
                for b in range(NX):
                    dve.wait_ge(rounded, i * NX + b + 1)
                    c = ds(i * NX + b, 1)
                    dve.tensor_tensor(xl[:, c, :], x[:, b:b + 1], xh[:, c, :].bitcast(F32),
                                      ALU.subtract).then_inc(x_free, 1)


class Weights:

    def __init__(self, st):
        self.raw = st.sb("w_raw", [P, 2, KC, P])
        self.hi = st.sb("w_hi", [P, 2, KC, P], F32R)
        self.lo = st.sb("w_lo", [P, 2, KC, P], F32R)
        self.loaded = [st.sem(f"w_loaded{b}") for b in range(2)]
        self.raw_free = st.sem("w_raw_free")
        self.split_free = st.sem("w_split_free")
        self.begun = st.sem("w_begun")
        self.ready = st.sem("w_ready")

    def load(self, sp, w_dram, n, i, b):
        sp.wait_ge(self.raw_free, n + 1)
        sp.dma_start(self.raw[:, b], w_dram[ds(n, 1)].rearrange("a p c m -> p (a c) m")).then_inc(self.loaded[b], 16)

    def split(self, pool, n, i, b):
        pool.wait_ge(self.loaded[b], i * 16 + 16)
        pool.wait_ge(self.split_free, n + 1)
        pool.sem_inc(self.begun, 1)
        pool.tensor_copy(self.hi[:, b], self.raw[:, b])
        pool.drain()
        pool.tensor_tensor(self.lo[:, b], self.raw[:, b], self.hi[:, b].bitcast(F32), ALU.subtract)
        pool.drain()
        pool.sem_inc(self.ready, 1)
        pool.sem_inc(self.raw_free, 1)

    def product(self, pe, out, b, xh, xl, m):
        g = slice(m * GW, (m + 1) * GW)
        for c in range(KC):
            pe.matmul(out, self.hi[:, b, c], xh[:, c, g], start=(c == 0), stop=False)
            pe.matmul(out, self.hi[:, b, c], xl[:, c, g], start=False, stop=False)
            mm = pe.matmul(out, self.lo[:, b, c], xh[:, c, g], start=False, stop=(c == KC - 1))
        return mm


def project(nc, name, w_dram, nblk, xh, xl, dst, residual=None, silu=False):
    with Stage(nc, name) as st:
        w = Weights(st)
        out = st.sb("out", [P, 2, T])
        res = st.sb("res", [P, 2, T]) if residual is not None else None
        acc = st.psum("acc", [P, NG, 512])
        product = st.sem("product")
        even_out, odd_out = st.sem("even_out"), st.sem("odd_out")
        stored = [st.sem(f"stored{b}") for b in range(2)]
        res_in = [st.sem(f"res_in{b}") for b in range(2)]
        block = st.block()
        npair, odd = nblk // 2, nblk % 2

        def blocks(eng, body):
            with eng.Fori(0, npair) as i:
                for b in range(2):
                    body(i * 2 + b, i, b)
            if odd:
                body(nblk - 1, npair, 0)

        @block.sync
        def _(sp):
            def body(n, i, b):
                w.load(sp, w_dram, n, i, b)
                if residual is not None:
                    sp.wait_ge(stored[b], i * 16 + 16)
                    sp.dma_start(res[:, b], residual[ds(n * P, P), :]).then_inc(res_in[b], 16)
            blocks(sp, body)

        @block.gpsimd
        def _(pool):
            pool.sem_inc(w.raw_free, 2)
            blocks(pool, lambda n, i, b: w.split(pool, n, i, b))

        @block.tensor
        def _(pe):
            pe.sem_inc(w.split_free, 2)

            def body(n, i, b):
                pe.wait_ge(w.ready, n + 1)
                for m in range(NG):
                    pe.wait_ge(odd_out if m % 2 else even_out, n * 3 + m // 2 + 1)
                    mm = w.product(pe, acc[:, m, 0:GW], b, xh, xl, m)
                    mm.then_inc(product, 1)
                pe.wait_ge(product, (n + 1) * NG)
                pe.sem_inc(w.split_free, 1)
            blocks(pe, body)

        def silu_of(dst_, src_):
            return nc.scalar.activation(dst_, src_, ACT.Silu)

        def copy_group(eng, copy, n, i, b, m, done):
            eng.wait_ge(product, n * NG + m + 1)
            if m < 2:
                eng.wait_ge(stored[b], i * 16 + 16)
            g = slice(m * GW, (m + 1) * GW)
            if residual is None:
                copy(out[:, b, g], acc[:, m, 0:GW]).then_inc(done, 1)
            else:
                if m < 2:
                    eng.wait_ge(res_in[b], i * 16 + 16)
                nc.vector.tensor_tensor(out[:, b, g], acc[:, m, 0:GW], res[:, b, g], ALU.add).then_inc(done, 1)

        @block.scalar
        def _(act):
            act.sem_inc(stored[0], 16)
            act.sem_inc(stored[1], 16)
            if residual is None:
                act.sem_inc(even_out, 3)
            if silu:
                act.sem_inc(odd_out, 3)

            def body(n, i, b):
                for m in range(NG):
                    if silu or (m % 2 == 0 and residual is None):
                        copy_group(act, silu_of if silu else nc.scalar.copy, n, i, b, m, odd_out if m % 2 else even_out)
                act.wait_ge(even_out, n * 3 + 6)
                act.wait_ge(odd_out, n * 3 + 6)
                act.dma_start(dst[ds(n * P, P), :], out[:, b]).then_inc(stored[b], 16)
            blocks(act, body)
            act.wait_ge(stored[0], 16 * (npair + odd + 1))
            act.wait_ge(stored[1], 16 * (npair + 1))

        @block.vector
        def _(dve):
            if silu:
                return
            dve.sem_inc(odd_out, 3)
            if residual is not None:
                dve.sem_inc(even_out, 3)

            def body(n, i, b):
                for m in range(NG):
                    if m % 2 or residual is not None:
                        copy_group(dve, nc.vector.tensor_copy, n, i, b, m, odd_out if m % 2 else even_out)
            blocks(dve, body)
GDN_TAPS, SC_TAPS = 4, 3


def prompt_and_samples(buf, taps):
    return buf[:, taps - 1:], buf[:, taps - 1 + SEQ:].rearrange("p (s t) -> p s t", s=NS)


def convolve(dve, y, x, xs, w, taps):
    ys = y[:, SEQ:].rearrange("p (s t) -> p s t", s=NS)
    for i in range(taps):
        for o, v in ((y[:, 0:SEQ], x[:, i:i + SEQ]), (ys, xs[:, :, i:i + TS])):
            if i == 0:
                ins = dve.tensor_scalar(o, v, w[:, 0:1], None, ALU.mult)
            else:
                ins = dve.scalar_tensor_tensor(o, v, w[:, i:i + 1], o, ALU.mult, ALU.add)
        if i < taps - 1:
            dve.drain()
    return ins


def project_gdn(nc, name, w_dram, par_dram, xh, xl, dst, tail_dram):
    H = GDN_TAPS - 1
    NPAR = NS * H + GDN_TAPS
    with Stage(nc, name) as st:
        w = Weights(st)
        x = st.sb("x", [P, H + T])
        xs = st.sb("xs", [P, NS, H + TS])
        y = st.sb("y", [P, 2, T])
        sq = st.sb("sq", [P, T])
        rstd = st.sb("rstd", [P, T])
        par = st.sb("par", [P, 2, NPAR])
        tail = st.sb("tail", [P, 2, H * (1 + NS)])
        ones, eps = st.sb("ones", [P, P]), st.sb("eps", [P, 1])
        acc = st.psum("acc", [P, NG, 512])
        ss = st.psum("ss", [P, 2, 512])
        const_set = st.sem("const_set")
        par_in = [st.sem(f"par_in{b}") for b in range(2)]
        product, copied = st.sem("product"), st.sem("copied")
        convolved = st.sem("convolved")
        activated = st.sem("activated")
        squared, summed, logs = st.sem("squared"), st.sem("summed"), st.sem("logs")
        rstd_set = st.sem("rstd_set")
        normed = st.sem("normed")
        tail_out = st.sem("tail_out")
        par_free = st.sem("par_free")
        stored = [st.sem(f"stored{b}") for b in range(2)]
        tail_stored = [st.sem(f"tail_stored{b}") for b in range(2)]
        block = st.block()
        NH2 = GH // 2
        blocks = [(j, j % 3, j // 3) for j in range(6)]

        @block.sync
        def _(sp):
            with sp.Fori(0, NH2) as i:
                for j, part, head in blocks:
                    n, b, k = i * 6 + j, j % 2, i * 3 + j // 2
                    w.load(sp, w_dram, n, k, b)
                    sp.wait_ge(par_free, n + 1)
                    sp.dma_start(par[:, b], par_dram[ds(n * P, P), :]).then_inc(par_in[b], 16)

        @block.gpsimd
        def _(pool):
            pool.sem_inc(w.raw_free, 2)
            with pool.Fori(0, NH2) as i:
                for j, part, head in blocks:
                    w.split(pool, i * 6 + j, i * 3 + j // 2, j % 2)

        @block.tensor
        def _(pe):
            pe.sem_inc(w.split_free, 2)
            pe.wait_ge(const_set, 2)

            def sums(i, head, part):
                k = i * 4 + head * 2 + part
                pe.wait_ge(squared, k + 1)
                for m in range(NG):
                    pe.wait_ge(logs, k * NG + m + 1)
                    pe.matmul(ss[:, m % 2, 0:GW], ones[:], sq[:, m * GW:(m + 1) * GW],
                              start=True, stop=True).then_inc(summed, 1)

            with pe.Fori(0, NH2) as i:
                for j, part, head in blocks:
                    n, b = i * 6 + j, j % 2
                    pe.wait_ge(w.ready, n + 1)
                    for m in range(NG):
                        if part and m == NG - 1:
                            sums(i, head, part - 1)
                        pe.wait_ge(copied, n * NG + m + 1)
                        w.product(pe, acc[:, m, 0:GW], b, xh, xl, m).then_inc(product, 1)
                    pe.wait_ge(product, (n + 1) * NG)
                    pe.sem_inc(w.split_free, 1)

        @block.scalar
        def _(act):
            act.sem_inc(copied, NG)
            act.sem_inc(logs, 2)
            for b in range(2):
                act.sem_inc(stored[b], 16)
                act.sem_inc(tail_stored[b], 16)
            act.wait_ge(const_set, 2)

            def roots(i, head, part):
                k = i * 4 + head * 2 + part
                for m in range(NG):
                    act.wait_ge(summed, k * NG + m + 1)
                    if m == 0:
                        act.wait_ge(normed, k + 1)
                    nc.scalar.activation(rstd[:, m * GW:(m + 1) * GW], ss[:, m % 2, 0:GW], ACT.Ln,
                                         bias=eps[:, 0:1]).then_inc(logs, 1)
                act.drain()
                nc.scalar.activation(rstd[:], rstd[:], ACT.Exp, scale=-0.5).then_inc(rstd_set, 1)

            def store(i, j, n):
                act.dma_start(dst[ds(n * P, P), :], y[:, j % 2]).then_inc(stored[j % 2], 16)

            with act.Fori(0, NH2) as i:
                for j, part, head in blocks:
                    n, b, k = i * 6 + j, j % 2, i * 3 + j // 2
                    act.wait_ge(convolved, n + 1)
                    for m in range(NG):
                        if part and m == NG - 1:
                            roots(i, head, part - 1)
                        act.wait_ge(product, n * NG + m + 1)
                        nc.scalar.copy(x[:, H + m * GW:H + (m + 1) * GW], acc[:, m, 0:GW]).then_inc(copied, 1)
                    act.wait_ge(tail_out, n + 1)
                    act.dma_start(tail_dram[ds(n * P, P), :], tail[:, b]).then_inc(tail_stored[b], 16)
                    act.wait_ge(convolved, n + 2)
                    nc.scalar.activation(y[:, b], y[:, b], ACT.Silu).then_inc(activated, 1)
                    act.wait_ge(activated, n + 1)
                    if part == 2:
                        store(i, j, n)
                    else:
                        nc.scalar.activation(sq[:], y[:, b], ACT.Square).then_inc(squared, 1)
                    if part:
                        act.wait_ge(normed, i * 4 + head * 2 + part + 1)
                        store(i, j - 1, n - 1)
            for b in range(2):
                act.wait_ge(stored[b], 16 * (3 * GH // 2 + 1))
                act.wait_ge(tail_stored[b], 16 * (3 * GH // 2 + 1))

        @block.vector
        def _(dve):
            dve.memset(ones[:], 1.0).then_inc(const_set, 1)
            dve.memset(eps[:], EPS).then_inc(const_set, 1)
            dve.memset(x[:, 0:H], 0.0)
            dve.drain()
            dve.sem_inc(convolved, 1)
            dve.sem_inc(normed, 1)
            dve.sem_inc(par_free, 2)
            _, own = prompt_and_samples(x, GDN_TAPS)

            def scale(i, head, part, b):
                k = i * 4 + head * 2 + part
                dve.wait_ge(rstd_set, k + 1)
                dve.scalar_tensor_tensor(y[:, b], y[:, b], P ** -0.5 if part == 0 else 1.0, rstd[:],
                                         ALU.mult, ALU.mult).then_inc(normed, 1)

            with dve.Fori(0, NH2) as i:
                for j, part, head in blocks:
                    n, b, k = i * 6 + j, j % 2, i * 3 + j // 2
                    dve.wait_ge(par_in[b], k * 16 + 16)
                    dve.tensor_copy(xs[:, :, 0:H], par[:, b, 0:NS * H].rearrange("p (s t) -> p s t", s=NS))
                    dve.wait_ge(copied, n * NG + 2 * NG)
                    dve.tensor_copy(xs[:, :, H:], own)
                    dve.drain()
                    dve.wait_ge(tail_stored[b], k * 16 + 16)
                    dve.tensor_copy(tail[:, b, 0:H], x[:, SEQ:SEQ + H])
                    dve.tensor_copy(tail[:, b, H:].rearrange("p (s t) -> p s t", s=NS),
                                    xs[:, :, TS:]).then_inc(tail_out, 1)
                    dve.wait_ge(stored[b], k * 16 + 16)
                    convolve(dve, y[:, b], x, xs, par[:, b, NS * H:], GDN_TAPS).then_inc(convolved, 1)
                    if part:
                        scale(i, head, part - 1, 1 - b)
                    dve.drain()
                    dve.sem_inc(par_free, 1)


def shortconv(nc, name, w_dram, par_dram, xh, xl, dst, tail_dram):
    H = SC_TAPS - 1
    NPAR = NS * H + SC_TAPS
    with Stage(nc, name) as st:
        w = Weights(st)
        u, gb, gz, y = (st.sb(s, [P, T]) for s in ("u", "gb", "gz", "y"))
        x = st.sb("x", [P, H + T])
        xs = st.sb("xs", [P, NS, H + TS])
        par = st.sb("par", [P, NPAR])
        tail = st.sb("tail", [P, H * (1 + NS)])
        acc = st.psum("acc", [P, NG, 512])
        par_in = st.sem("par_in")
        product = st.sem("product")
        u_out, gb_out, gz_out = st.sem("u_out"), st.sem("gb_out"), st.sem("gz_out")
        cu_out = st.sem("cu_out")
        convolved, gated = st.sem("convolved"), st.sem("gated")
        tail_out = st.sem("tail_out")
        stored, tail_stored = st.sem("stored"), st.sem("tail_stored")
        block = st.block()
        NJ = D // P

        @block.sync
        def _(sp):
            with sp.Fori(0, NJ) as i:
                for part in range(4):
                    w.load(sp, w_dram, i * 4 + part, i * 2 + part // 2, part % 2)
                sp.wait_ge(tail_stored, i * 16 + 16)
                sp.wait_ge(stored, i * 16 + 16)
                sp.dma_start(par[:], par_dram[ds(i * P, P), :]).then_inc(par_in, 16)

        @block.gpsimd
        def _(pool):
            pool.sem_inc(w.raw_free, 2)
            with pool.Fori(0, NJ) as i:
                for part in range(4):
                    w.split(pool, i * 4 + part, i * 2 + part // 2, part % 2)

        @block.tensor
        def _(pe):
            pe.sem_inc(w.split_free, 2)
            with pe.Fori(0, NJ) as i:
                for part in range(4):
                    n = i * 4 + part
                    pe.wait_ge(w.ready, n + 1)
                    for m in range(NG):
                        before, start = [(gz_out, 0), (u_out, 0), (gb_out, 0), (cu_out, NG)][part]
                        pe.wait_ge(before, i * NG + start + m + 1)
                        w.product(pe, acc[:, m, 0:GW], part % 2, xh, xl, m).then_inc(product, 1)
                    pe.wait_ge(product, (n + 1) * NG)
                    pe.sem_inc(w.split_free, 1)

        def group(m):
            return slice(m * GW, (m + 1) * GW)

        @block.scalar
        def _(act):
            act.sem_inc(gz_out, NG)
            act.sem_inc(stored, 16)
            act.sem_inc(tail_stored, 16)
            with act.Fori(0, NJ) as i:
                act.wait_ge(cu_out, i * NG + NG)
                for m in range(NG):
                    act.wait_ge(product, i * 4 * NG + m + 1)
                    nc.scalar.copy(u[:, group(m)], acc[:, m, 0:GW]).then_inc(u_out, 1)
                act.wait_ge(gated, i * 1 + 1)
                for m in range(NG):
                    act.wait_ge(product, (i * 4 + 1) * NG + m + 1)
                    nc.scalar.copy(gb[:, group(m)], acc[:, m, 0:GW]).then_inc(gb_out, 1)
                for m in range(NG):
                    act.wait_ge(product, (i * 4 + 3) * NG + m + 1)
                    nc.scalar.activation(gz[:, group(m)], acc[:, m, 0:GW], ACT.Silu).then_inc(gz_out, 1)
                act.wait_ge(tail_out, i + 1)
                act.dma_start(tail_dram[ds(i * P, P), :], tail[:]).then_inc(tail_stored, 16)
                act.wait_ge(gated, i + 2)
                act.dma_start(dst[ds(i * P, P), :], y[:]).then_inc(stored, 16)
            act.wait_ge(stored, 16 * (NJ + 1))
            act.wait_ge(tail_stored, 16 * (NJ + 1))

        @block.vector
        def _(dve):
            dve.memset(x[:, 0:H], 0.0)
            dve.drain()
            dve.sem_inc(cu_out, NG)
            dve.sem_inc(gated, 1)
            _, own = prompt_and_samples(x, SC_TAPS)
            with dve.Fori(0, NJ) as i:
                for m in range(NG):
                    dve.wait_ge(u_out, i * NG + m + 1)
                    dve.wait_ge(product, (i * 4 + 2) * NG + m + 1)
                    dve.tensor_tensor(x[:, H + m * GW:H + (m + 1) * GW], acc[:, m, 0:GW], u[:, group(m)],
                                      ALU.mult).then_inc(cu_out, 1)
                dve.drain()
                dve.wait_ge(par_in, i * 16 + 16)
                dve.tensor_copy(xs[:, :, 0:H], par[:, 0:NS * H].rearrange("p (s t) -> p s t", s=NS))
                dve.tensor_copy(xs[:, :, H:], own)
                dve.drain()
                dve.tensor_copy(tail[:, 0:H], x[:, SEQ:SEQ + H])
                dve.tensor_copy(tail[:, H:].rearrange("p (s t) -> p s t", s=NS), xs[:, :, TS:]).then_inc(tail_out, 1)
                dve.wait_ge(stored, i * 16 + 16)
                convolve(dve, y, x, xs, par[:, NS * H:], SC_TAPS)
                dve.drain()
                dve.wait_ge(gb_out, i * NG + NG)
                dve.tensor_tensor(y[:], y[:], gb[:], ALU.mult)
                dve.drain()
                dve.wait_ge(gz_out, i * NG + 2 * NG)
                dve.tensor_tensor(y[:], y[:], gz[:], ALU.mult).then_inc(gated, 1)
                dve.drain()
def constants():
    k, q = np.arange(P)[:, None], np.arange(P)[None, :]
    own = (k // TS == q // TS) & (k < NS * TS) & (q < NS * TS)
    level = lambda s: (k // (2 * s) == q // (2 * s)) & (k // s != q // s) & (k > q)
    mats = dict(
        ident=k == q,
        suffix=-1.0 * (k >= q),
        earlier=k < q,
        not_earlier=-1e30 * (k >= q),
        upto=k <= q,
        later=-1e30 * (k > q),
        upto_own=(k <= q) & own,
        later_own=-1e30 * ~((k <= q) & own),
        low16=(k // 16 == q // 16) & (k > q),
        up16=(k // 16 == q // 16) & (k < q),
        level16=level(16), level32=level(32), level64=level(64),
    )
    assert list(mats) == CONST
    return np.stack([m.astype(np.float32) for m in mats.values()], 1)


CONST = ["ident", "suffix", "earlier", "not_earlier", "upto", "later", "upto_own", "later_own",
         "low16", "up16", "level16", "level32", "level64"]


def const(dram, name):
    return dram[:, CONST.index(name)]


def softplus(nc, act, z, t):
    nc.scalar.activation(t, z, ACT.Abs)
    act.drain()
    nc.scalar.activation(t, t, ACT.Exp, scale=-1.0)
    act.drain()
    return nc.scalar.activation(t, t, ACT.Ln, bias=1.0)


def prompt_attention(nc, name, proj, bias_dram, const_dram, mix):
    DB = SBD + 2
    GQ = 512
    NKG = GQ // P
    NGQ = SEQ // GQ
    NB = SEQ // P
    head_steps = [(g, kb) for g in range(NGQ) for kb in range(NKG * (g + 1) - 1, -1, -1)]
    NSTEP = len(head_steps)
    steps = [(b, g, kb) for b in range(2) for g, kb in head_steps]
    N2 = len(steps)
    NPAIR = SBH // 2
    assert N2 % 4 == 0
    with Stage(nc, name) as st:
        q_raw, k_raw = st.sb("q_raw", [P, 2, SEQ]), st.sb("k_raw", [P, 2, SEQ])
        k_pair, q_twice = (st.sb(s, [P, 2, SEQ], F32R) for s in ("k_pair", "q_twice"))
        k_high, q_low = (st.sb(s, [DB, 2, SEQ], F32R) for s in ("k_high", "q_low"))
        v, gate = st.sb("v", [SBD, 2, SEQ]), st.sb("gate", [SBD, 2, SEQ])
        vt_hi, vt_lo = (st.sb(s, [P, 2, NB, SBD], F32R) for s in ("vt_hi", "vt_lo"))
        bias, bias_lo, bias_pair = (st.sb(s, [DB, SBH]) for s in ("bias", "bias_lo", "bias_pair"))
        bias_hi = st.sb("bias_hi", [DB, SBH], F32R)
        ones = st.sb("ones", [DB, GQ])
        ident, suffix, earlier, masked, minus = (st.sb(s, [P, P]) for s in
                                                 ("ident", "suffix", "earlier", "masked", "minus"))
        suffix_r = st.sb("suffix_r", [P, P], F32R)
        t = st.sb("t", [P, 2, GQ])
        sp_hi, sp_lo = (st.sb(s, [P, 2, GQ], F32R) for s in ("sp_hi", "sp_lo"))
        a, sp, acc = (st.sb(s, [P, 4, GQ]) for s in ("a", "sp", "acc"))
        a_hi, a_lo = (st.sb(s, [P, 4, GQ], F32R) for s in ("a_hi", "a_lo"))
        o = st.sb("o", [SBD, 2, GQ])
        z = st.psum("z", [P, 4, 512])
        out = st.psum("out", [SBD, 2, 512])
        vps = st.psum("vps", [P, 2, 512])
        const_in, const_set = st.sem("const_in"), st.sem("const_set")
        loaded = [[st.sem(f"loaded_{s}{b}") for b in range(2)] for s in "qkvz"]
        head_read = [st.sem(f"head_read{b}") for b in range(2)]
        gate_read = [st.sem(f"gate_read{b}") for b in range(2)]
        rounded = st.sem("rounded")
        split = st.sem("split")
        turned = st.sem("turned")
        vt_out = st.sem("vt_out")
        scores = st.sem("scores")
        logs = st.sem("logs")
        plus = st.sem("plus")
        summed = st.sem("summed")
        carried = st.sem("carried")
        weights = st.sem("weights")
        a_rounded = st.sem("a_rounded")
        begun = st.sem("begun")
        a_split = st.sem("a_split")
        used = st.sem("used")
        gated = st.sem("gated")
        stored, o_free = st.sem("stored"), st.sem("o_free")
        turning = st.sem("turning")
        block = st.block()

        def columns(g, kb):
            c = max(0, kb - NKG * g) * P
            return c, kb >= NKG * g

        def pairs(eng, body):
            with eng.Fori(0, NPAIR - 1) as i:
                body(i, False)
            body(NPAIR - 1, True)

        @block.sync
        def _(sync):
            for dst, s in ((ident, "ident"), (suffix, "suffix"), (earlier, "earlier"), (masked, "not_earlier")):
                sync.dma_start(dst[:], const(const_dram, s)).then_inc(const_in, 16)
            for row in range(2):
                sync.dma_start(bias[SBD + row:SBD + row + 1], bias_dram).then_inc(const_in, 16)

            def load(i, b):
                sync.wait_ge(head_read[b], i + 1)
                sync.wait_ge(gate_read[b], i + 1)
                for s, (dst, row) in enumerate(((q_raw, Q0), (k_raw, K0), (v, V0), (gate, Z0))):
                    for half in range(2 if s < 2 else 1):
                        sync.dma_start(dst[half * SBD:(half + 1) * SBD, b],
                                       proj[ds((i * 2 + b) * SBD + row * P, SBD), 0:SEQ]).then_inc(loaded[s][b], 16)

            def body(i, last):
                for b in range(2):
                    for g in range(NGQ):
                        n = i * 2 * NGQ + b * NGQ + g
                        sync.wait_ge(gated, n + 3)
                        sync.dma_start(mix[ds((i * 2 + b) * SBD, SBD), g * GQ:(g + 1) * GQ],
                                       o[:, g % 2]).then_inc(stored, 16)
                        sync.wait_ge(stored, n * 16 + 16)
                        sync.sem_inc(o_free, 1)
                    if not last:
                        load(i + 1, b)

            sync.sem_inc(o_free, 2)
            load(0, 0)
            load(0, 1)
            pairs(sync, body)

        @block.gpsimd
        def _(pool):
            pool.sem_inc(a_split, 4)
            pool.sem_inc(summed, 4)

            def add_up(i, s):
                c, diagonal = columns(*steps[s][1:])
                c1 = c + P if diagonal else c
                pool.wait_ge(plus, i * N2 + s + 3)
                pool.sem_inc(begun, 1)
                if diagonal:
                    pool.tensor_copy(acc[:, s % 4, c:c + P], sp[:, s % 4, c:c + P])
                if c1 < GQ:
                    pool.tensor_tensor(acc[:, s % 4, c1:GQ], acc[:, (s - 1) % 4, c1:GQ], sp[:, s % 4, c1:GQ], ALU.add)
                pool.drain()
                pool.sem_inc(summed, 1)

            def split_a(i, s):
                c, _ = columns(*steps[s][1:])
                pool.wait_ge(a_rounded, i * N2 + s + 1)
                pool.tensor_tensor(a_lo[:, s % 4, c:GQ], a[:, s % 4, c:GQ], a_hi[:, s % 4, c:GQ].bitcast(F32),
                                   ALU.subtract).then_inc(a_split, 1)

            def body(i, last):
                for s in range(N2 + 3):
                    if s < N2:
                        add_up(i, s)
                    if s >= 3:
                        split_a(i, s - 3)
            pairs(pool, body)

        @block.tensor
        def _(pe):
            pe.sem_inc(carried, 2)
            pe.sem_inc(used, 4)
            pe.sem_inc(head_read[0], 1)
            pe.sem_inc(head_read[1], 1)
            pe.wait_ge(const_in, 16 * 6)
            pe.wait_ge(const_set, 1)

            def turn_v(i, b):
                pe.wait_ge(loaded[2][b], i * 16 + 16)
                pe.wait_ge(vt_out, i * 2 + b + 1)
                pe.sem_inc(turning, 1)
                for kb in range(NB):
                    mm = pe.transpose(vps[:, kb // 8, (kb % 8) * SBD:(kb % 8 + 1) * SBD],
                                      v[:, b, kb * P:(kb + 1) * P], ident[0:SBD, 0:SBD])
                mm.then_inc(turned, 1)

            def score(i, s):
                b, g, kb = steps[s]
                c, _ = columns(g, kb)
                if s % NSTEP == 0:
                    pe.wait_ge(split, i * 2 + b + 1)
                pe.wait_ge(weights, i * N2 + s + 1)
                keys, queries = slice(kb * P, (kb + 1) * P), slice(g * GQ + c, (g + 1) * GQ)
                pe.matmul(z[:, s % 4, c:GQ], k_pair[:, b, keys], q_twice[:, b, queries], start=True, stop=False)
                pe.matmul(z[:, s % 4, c:GQ], k_high[:, b, keys], q_low[:, b, queries], start=False, stop=True
                          ).then_inc(scores, 1)

            def carry(i, s):
                b, g, kb = steps[s]
                c, diagonal = columns(g, kb)
                c1 = c + P if diagonal else c
                pe.wait_ge(plus, i * N2 + s + 3)
                for part in (sp_hi, sp_lo):
                    mm = pe.matmul(z[:, s % 4, c:GQ], suffix_r[:], part[:, s % 2, c:GQ], start=False, stop=True,
                                   skip_group_check=True)
                if diagonal:
                    mm = pe.matmul(z[:, s % 4, c:c + P], ident[:], masked[:], start=False, stop=True,
                                   skip_group_check=True)
                if c1 < GQ:
                    pe.wait_ge(summed, i * N2 + s + 4)
                    mm = pe.matmul(z[:, s % 4, c1:GQ], minus[:], acc[:, (s - 1) % 4, c1:GQ], start=False,
                                   stop=True, skip_group_check=True)
                mm.then_inc(carried, 1)

            def apply(i, s):
                b, g, kb = steps[s]
                c, _ = columns(g, kb)
                if s % NSTEP == 0:
                    pe.wait_ge(vt_out, i * 2 + b + 2)
                first = kb == NKG * (g + 1) - 1
                if first:
                    pe.wait_ge(gated, i * 2 * NGQ + b * NGQ + g + 1)
                pe.wait_ge(a_split, i * N2 + s + 5)
                for n, (v_, a_) in enumerate(((vt_hi, a_hi), (vt_lo, a_hi), (vt_hi, a_lo))):
                    mm = pe.matmul(out[:, g % 2, c:GQ], v_[:, b, kb], a_[:, s % 4, c:GQ],
                                   start=(first and n == 0), stop=(kb == 0 and n == 2), skip_group_check=True)
                mm.then_inc(used, 1)
                if s % NSTEP == NSTEP - 1:
                    pe.wait_ge(used, i * N2 + s + 5)
                    pe.sem_inc(head_read[b], 1)

            def body(i, last):
                for s in range(N2 + 5):
                    if s == NSTEP // 2:
                        turn_v(i, 1)
                    if s == NSTEP + NSTEP // 2 and not last:
                        turn_v(i + 1, 0)
                    if s < N2:
                        score(i, s)
                    if 2 <= s < N2 + 2:
                        carry(i, s - 2)
                    if s >= 5:
                        apply(i, s - 5)
            turn_v(0, 0)
            pairs(pe, body)

        @block.scalar
        def _(act):
            nc.scalar.preload_act_table_set("natural_log_exp_and_others")
            act.sem_inc(weights, 4)

            def round_head(i, b, piece):
                act.wait_ge(loaded[0 if piece == 0 else 1][b], i * 32 + 32)
                if piece == 0:
                    ins = nc.scalar.mul(q_twice[:, b], q_raw[:, b], SBD ** -0.5)
                elif piece == 1:
                    ins = nc.scalar.copy(k_pair[:, b], k_raw[:, b])
                else:
                    ins = nc.scalar.copy(k_high[0:SBD, b], k_raw[0:SBD, b])
                ins.then_inc(rounded, 1)

            def body(i, last):
                for s in range(N2 + 2):
                    for piece in range(3):
                        if s == NSTEP // 2 + piece * 3:
                            round_head(i, 1, piece)
                        if s == NSTEP + NSTEP // 2 + piece * 3 and not last:
                            round_head(i + 1, 0, piece)
                    if s < N2:
                        b, g, kb = steps[s]
                        c, _ = columns(g, kb)
                        act.wait_ge(scores, i * N2 + s + 1)
                        act.wait_ge(plus, i * N2 + s + 1)
                        softplus(nc, act, z[:, s % 4, c:GQ], t[:, s % 2, c:GQ]).then_inc(logs, 1)
                    if s >= 2:
                        r = s - 2
                        c, _ = columns(*steps[r][1:])
                        act.wait_ge(carried, i * N2 + r + 3)
                        act.wait_ge(a_split, i * N2 + r + 1)
                        nc.scalar.activation(a[:, r % 4, c:GQ], z[:, r % 4, c:GQ], ACT.Exp).then_inc(weights, 1)
            for piece in range(3):
                round_head(0, 0, piece)
            pairs(act, body)

        @block.vector
        def _(dve):
            dve.memset(minus[:], -1.0)
            dve.memset(ones[SBD:DB], 1.0)
            dve.drain()
            for b in range(2):
                for g in range(NGQ):
                    dve.tensor_copy(q_low[SBD:DB, b, g * GQ:(g + 1) * GQ], ones[SBD:DB])
            dve.sem_inc(plus, 2)
            dve.sem_inc(gated, 2)
            dve.sem_inc(vt_out, 1)
            dve.sem_inc(gate_read[0], 1)
            dve.sem_inc(gate_read[1], 1)
            dve.wait_ge(const_in, 16 * 6)
            dve.tensor_copy(suffix_r[:], suffix[:])
            r = slice(SBD, DB)
            dve.tensor_copy(bias_hi[r], bias[r])
            dve.drain()
            dve.tensor_tensor(bias_lo[r], bias[r], bias_hi[r].bitcast(F32), ALU.subtract)
            dve.drain()
            dve.tensor_scalar(bias_lo[r], bias_lo[r], ident[r, SBD + 1:SBD + 2], None, ALU.mult)
            dve.drain()
            dve.scalar_tensor_tensor(bias_pair[r], bias_hi[r].bitcast(F32), ident[r, SBD:SBD + 1], bias_lo[r],
                                     ALU.mult, ALU.add)
            dve.drain()
            dve.sem_inc(const_set, 1)

            def split_head(i, b, piece):
                hi, lo = (m[:, b].rearrange("p (a n) d -> p a (n d)", a=2) for m in (vt_hi, vt_lo))
                if piece == 0:
                    dve.wait_ge(rounded, i * 6 + b * 3 + 1)
                    dve.scalar_tensor_tensor(q_low[0:SBD, b], q_raw[0:SBD, b], SBD ** -0.5,
                                             q_twice[0:SBD, b].bitcast(F32), ALU.mult, ALU.subtract)
                elif piece == 1:
                    dve.wait_ge(rounded, i * 6 + b * 3 + 2)
                    dve.tensor_tensor(k_pair[SBD:P, b], k_raw[SBD:P, b], k_pair[SBD:P, b].bitcast(F32), ALU.subtract)
                elif piece == 2:
                    dve.wait_ge(rounded, i * 6 + b * 3 + 3)
                    dve.tensor_scalar(k_high[r, b], q_low[r, b].bitcast(F32), bias_pair[r, ds(i * 2 + b, 1)], None, ALU.mult)
                    dve.drain()
                    dve.sem_inc(split, 1)
                else:
                    dve.wait_ge(turned, i * 2 + b + 1)
                    dve.wait_ge(head_read[b], i + 1)
                    dve.tensor_copy(hi, vps[:])
                    dve.drain()
                    dve.tensor_tensor(lo, vps[:], hi.bitcast(F32), ALU.subtract).then_inc(vt_out, 1)

            def round_a(i, s):
                c, _ = columns(*steps[s][1:])
                dve.wait_ge(weights, i * N2 + s + 5)
                dve.wait_ge(used, i * N2 + s + 1)
                dve.tensor_copy(a_hi[:, s % 4, c:GQ], a[:, s % 4, c:GQ]).then_inc(a_rounded, 1)

            def gate_group(i, s):
                b, g, _ = steps[s]
                dve.wait_ge(used, i * N2 + s + 5)
                if g == 0:
                    dve.wait_ge(loaded[3][b], i * 16 + 16)
                dve.wait_ge(o_free, i * 2 * NGQ + b * NGQ + g + 1)
                dve.tensor_tensor(o[:, g % 2], out[:, g % 2], gate[:, b, g * GQ:(g + 1) * GQ],
                                  ALU.mult).then_inc(gated, 1)
                if g == NGQ - 1:
                    dve.drain()
                    dve.sem_inc(gate_read[b], 1)

            def body(i, last):
                for s in range(N2):
                    b, g, kb = steps[s]
                    c, diagonal = columns(g, kb)
                    for piece in range(4):
                        if s == NSTEP // 2 + 2 + piece * 3:
                            split_head(i, 1, piece)
                        if s == NSTEP + NSTEP // 2 + 2 + piece * 3 and not last:
                            split_head(i + 1, 0, piece)
                    sp_s = sp[:, s % 4, c:GQ]
                    dve.wait_ge(logs, i * N2 + s + 1)
                    dve.wait_ge(carried, i * N2 + s + 1)
                    dve.wait_ge(summed, i * N2 + s + 1)
                    dve.scalar_tensor_tensor(sp_s, z[:, s % 4, c:GQ], 0.0, t[:, s % 2, c:GQ], ALU.max, ALU.add)
                    dve.drain()
                    if diagonal:
                        dve.tensor_tensor(sp[:, s % 4, c:c + P], sp[:, s % 4, c:c + P], earlier[:], ALU.mult)
                        dve.drain()
                    dve.tensor_copy(sp_hi[:, s % 2, c:GQ], sp_s)
                    dve.drain()
                    dve.tensor_tensor(sp_lo[:, s % 2, c:GQ], sp_s, sp_hi[:, s % 2, c:GQ].bitcast(F32), ALU.subtract
                                      ).then_inc(plus, 1)
                    if s >= 3:
                        round_a(i, s - 3)
                    if s >= 6 and steps[s - 6][2] == 0:
                        gate_group(i, s - 6)
                for s in range(N2 - 3, N2):
                    round_a(i, s)
                gate_group(i, N2 - 1)
            for piece in range(4):
                split_head(0, 0, piece)
            pairs(dve, body)


def own_rows():
    return (np.arange(P)[:, None] // TS == np.arange(NS)[None]).astype(np.float32)
def head_constants():
    r = np.arange(SBH * TS)[:, None]
    return np.concatenate([r // TS == np.arange(SBH * SBD)[None] // SBD, r % TS == np.arange(TS)[None]],
                          1).astype(np.float32)


def sample_attention(nc, name, proj, bias_dram, bias_rows_dram, pages_dram, k_pool, v_pool, const_dram, heads_dram, mix):
    NP = 8
    NB = NPAGE // NP
    NX = NS * NB
    HQ = SBH * TS
    NC = SBH // 2
    C2 = 2 * TS
    W = NP * HQ
    assert W == 512 and NS * HQ == 512
    with Stage(nc, name) as st:
        kp = st.sb("kp", [P, 2, NP, NC, PAGE])
        vp = st.sb("vp", [P, 2, NP, NC * P])
        v_hi, v_lo = st.sb("v_hi", [P, 2, NP, NC * P], F32R), st.sb("v_lo", [P, NP, NC * P], F32R)
        table = st.sb("table", [1, NX * NP], I32)
        qn, kn, vn, zn = (st.sb(s, [P, NC, NS * TS]) for s in ("qn", "kn", "vn", "zn"))
        qb = st.sb("qb", [P, NS, NC, HQ])
        q_now = st.sb("q_now", [P, 2, NC, HQ])
        heads = st.sb("heads", [2 * HQ, NC * P])
        pick = st.sb("pick", [2 * HQ, TS])
        vt = st.sb("vt", [TS, NS, NC * P])
        bias = st.sb("bias", [1, SBH])
        bias_rows = st.sb("bias_rows", [HQ, 1])
        zb = st.sb("zb", [HQ, NP * PAGE])
        bias_row = st.sb("bias_row", [1, NP, SBH, TS])
        ones_row = st.sb("ones_row", [1, P])
        ident, suffix, earlier, masked, minus = (st.sb(s, [P, P]) for s in
                                                 ("ident", "suffix", "earlier", "masked", "minus"))
        mask_new = st.sb("mask_new", [TS, W])
        t, sp, acc, a = (st.sb(s, [P, 2, W]) for s in ("t", "sp", "acc", "a"))
        a_pair = st.sb("a_pair", [P, 2, NP, 2, HQ], F32R)
        carry_in = st.sb("carry_in", [P, NS, HQ])
        total = st.sb("total", [2 * HQ, NS, NC * P])
        o = st.sb("o", [P, NC, NS * TS])
        z = st.psum("z", [P, 2, 512])
        out = st.psum("out", [P, 2, 512])
        zq = st.psum("zq", [HQ, 2, 512])
        vps = st.psum("vps", [P, 2, 512])
        table_in, proj_in, const_in = st.sem("table_in"), st.sem("proj_in"), st.sem("const_in")
        k_in = [[st.sem(f"k_in{b}{half}") for half in range(2)] for b in range(2)]
        v_in = [st.sem(f"v_in{b}") for b in range(2)]
        k_read, v_read, v_read_pool = (st.sem(s) for s in ("k_read", "v_read", "v_read_pool"))
        ready = st.sem("ready")
        turned, vt_out = st.sem("turned"), st.sem("vt_out")
        masked_out = st.sem("masked_out")
        new_scores, new_logs, new_plus, new_carried, new_weights, new_used, new_done = (
            st.sem(f"new_{s}") for s in ("scores", "logs", "plus", "carried", "weights", "used", "done"))
        scores, logs = st.sem("scores"), st.sem("logs")
        q_set = st.sem("q_set")
        biased, z_turned = st.sem("biased"), st.sem("z_turned")
        turning = st.sem("turning")
        v_rounded = st.sem("v_rounded")
        v_split, v_split_pool = st.sem("v_split"), st.sem("v_split_pool")
        VD = 5
        exps, a_taken = st.sem("exps"), st.sem("a_taken")
        plus, summed = st.sem("plus"), st.sem("summed")
        carried, weights, used, added = (st.sem(s) for s in ("carried", "weights", "used", "added"))
        stored = st.sem("stored")
        block = st.block()
        new = slice(SEQ, T)

        @block.sync
        def _(sp_):
            sp_.dma_start(table[:], pages_dram).then_inc(table_in, 16)
            for dst, row in ((qn, Q0), (kn, K0), (vn, V0), (zn, Z0)):
                sp_.dma_start(dst[:], proj[row * P:(row + NC) * P, new].rearrange("(c p) t -> p c t", p=P)
                              ).then_inc(proj_in, 16)
            for dst, s in ((ident, "ident"), (suffix, "suffix"), (earlier, "earlier"), (masked, "not_earlier")):
                sp_.dma_start(dst[:], const(const_dram, s)).then_inc(const_in, 16)
            sp_.dma_start(bias[:], bias_dram).then_inc(const_in, 16)
            sp_.dma_start(bias_rows[:], bias_rows_dram).then_inc(const_in, 16)
            for part in range(2):
                rows = slice(part * HQ, (part + 1) * HQ)
                sp_.dma_start(heads[rows], heads_dram[:, 0:NC * P]).then_inc(const_in, 16)
                sp_.dma_start(pick[rows], heads_dram[:, NC * P:]).then_inc(const_in, 16)
            sp_.wait_ge(table_in, 16)
            with sp_.Fori(0, NX // 2) as i:
                pages = []
                for b in range(2):
                    x = i * 2 + b
                    pages += [[sp_.value_load(table[0:1, ds(x * NP + p, 1)], min_val=0,
                                              max_val=k_pool.shape[0] - 1) for p in range(NP)]]
                    sp_.wait_ge(k_read, x + 1)
                    for p in range(NP):
                        sp_.dma_start(kp[:, b, p], k_pool[ds(pages[b][p], 1)].rearrange("a p c k -> p (a c) k")
                                      ).then_inc(k_in[b][p // (NP // 2)], 16)
                for b in range(2):
                    sp_.wait_ge(v_read, i * 2 + b + 1)
                    sp_.wait_ge(v_read_pool, i * 2 + b + 1)
                    for p in range(NP):
                        sp_.dma_start(vp[:, b, p], v_pool[ds(pages[b][p], 1)].rearrange(
                            "a k e -> k (a e)")).then_inc(v_in[b], 16)
            sp_.wait_ge(new_done, 1)
            sp_.dma_start(mix[0:NC * P, new].rearrange("(c p) t -> p c t", p=P), o[:]).then_inc(stored, 16)
            sp_.wait_ge(stored, 16)

        @block.tensor
        def _(pe):
            pe.sem_inc(k_read, 2)
            pe.sem_inc(carried, 2)
            pe.sem_inc(used, 2)
            pe.wait_ge(const_in, 16 * 10)
            pe.wait_ge(proj_in, 16 * 4)
            for two in range(NS // 2):
                if two:
                    pe.wait_ge(vt_out, two)
                for s in range(2):
                    for c in range(NC):
                        mm = pe.transpose(vps[0:TS, s, c * P:(c + 1) * P],
                                          vn[:, c, (two * 2 + s) * TS:(two * 2 + s + 1) * TS], ident[:])
                mm.then_inc(turned, 1)
            pe.wait_ge(ready, 1)
            pe.matmul(z[0:TS, 0], ones_row[:, 0:TS], bias_row[:].rearrange("a p h q -> a (p h q)"), start=True,
                      stop=False, skip_group_check=True)
            for s in range(NS):
                for c in range(NC):
                    col = s * HQ + c * C2
                    mm = pe.matmul(z[0:TS, 0, col:col + C2], kn[:, c, s * TS:(s + 1) * TS],
                                   qb[:, s, c, c * C2:(c + 1) * C2],
                                   start=False, stop=True, skip_group_check=True)
            mm.then_inc(new_scores, 1)
            pe.wait_ge(new_plus, 1)
            pe.matmul(z[0:TS, 0], suffix[0:TS, 0:TS], sp[0:TS, 0], start=False, stop=True, skip_group_check=True)
            pe.matmul(z[0:TS, 0], ident[0:TS, 0:TS], mask_new[:], start=False, stop=True,
                      skip_group_check=True).then_inc(new_carried, 1)
            pe.wait_ge(new_weights, 1)
            pe.wait_ge(vt_out, NS // 2)
            for s in range(NS):
                pe.wait_ge(added, s + 1)
                pe.matmul(out[0:HQ, s % 2], a[0:TS, 0, s * HQ:(s + 1) * HQ], vt[:, s],
                          start=True, stop=True).then_inc(new_used, 1)

            def score(x, i, b, half):
                if half == 0:
                    pe.wait_ge(q_set, x + 1)
                    if not isinstance(x, int) or x:
                        pe.wait_ge(biased, x)
                pe.wait_ge(k_in[b][half], (i + 1) * (8 * NP))
                for c in range(NC):
                    mm = pe.matmul(zq[:, half].rearrange("r (p k) -> r p k", k=PAGE), q_now[:, b, c],
                                   kp[:, b, half * (NP // 2):(half + 1) * (NP // 2), c],
                                   start=(c == 0), stop=(c == NC - 1))
                if half:
                    mm.then_inc(scores, 1)
                    pe.wait_ge(scores, x + 1)
                    pe.sem_inc(k_read, 1)

            def turn(x, b):
                pe.wait_ge(biased, x + 1)
                pe.wait_ge(weights, x + 1)
                pe.sem_inc(turning, 1)
                for p in range(NP):
                    mm = pe.matmul(z[:, b, p * HQ:(p + 1) * HQ], zb[:, p * PAGE:(p + 1) * PAGE],
                                   ident[0:HQ, 0:HQ], is_transpose=True, start=(p == 0), stop=True,
                                   skip_group_check=True)
                mm.then_inc(z_turned, 1)

            def carry(x, b):
                pe.wait_ge(plus, x + 3)
                pe.matmul(z[:, b], suffix[:], sp[:, b], start=False, stop=True, skip_group_check=True)
                pe.wait_ge(summed, x + 1)
                pe.matmul(z[:, b], minus[:], acc[:, b], start=False, stop=True,
                          skip_group_check=True).then_inc(carried, 1)

            def apply(x, b, half):
                if half == 0:
                    pe.wait_ge(v_split, x + 1)
                    pe.wait_ge(v_split_pool, x + 1)
                    pe.wait_ge(added, NS + x + 1)
                    pe.wait_ge(weights, x + 3)
                for p in range(half * (NP // 2), (half + 1) * (NP // 2)):
                    pe.matmul(out[:, b], a_pair[:, b, p].rearrange("k a r -> k (a r)"), v_hi[:, b, p],
                              start=(p == 0), stop=False, skip_group_check=True)
                    mm = pe.matmul(out[0:HQ, b], a_pair[:, b, p, 0], v_lo[:, p],
                                   start=False, stop=(p == NP - 1), skip_group_check=True)
                if half:
                    mm.then_inc(used, 1)

            def step(x, i, b):
                score(x + 1, i, b, 0)
                carry(x, 1 - b)
                score(x + 1, i, b, 1)
                apply(x, 1 - b, 0)
                turn(x + 1, b)
                apply(x, 1 - b, 1)

            score(0, 0, 0, 0)
            score(0, 0, 0, 1)
            turn(0, 0)
            with pe.Fori(0, NX // 2 - 1) as i:
                step(i * 2, i, 1)
                step(i * 2 + 1, i + 1, 0)
            step(NX - 2, NX // 2 - 1, 1)
            carry(NX - 1, 1)
            apply(NX - 1, 1, 0)
            apply(NX - 1, 1, 1)
            pe.wait_ge(masked_out, 1)
            for c in range(NC):
                for s in range(NS):
                    col = (c * NS + s) * TS
                    mm = pe.matmul(vps[:, 0, col:col + TS], total[:, s, c * P:(c + 1) * P], pick[:],
                                   start=True, stop=True)
            mm.then_inc(turned, 1)

        @block.gpsimd
        def _(pool):
            pool.sem_inc(v_read_pool, 2)
            with pool.Fori(0, NX // 2) as i:
                for b in range(2):
                    x = i * 2 + b
                    pool.wait_ge(v_rounded, x + 1)
                    pool.wait_ge(used, x + 2)
                    pool.tensor_tensor(v_lo[:, VD:], vp[:, b, VD:], v_hi[:, b, VD:].bitcast(F32), ALU.subtract
                                       ).then_inc(v_split_pool, 1)
                    pool.drain()
                    pool.sem_inc(v_read_pool, 1)

        @block.scalar
        def _(act):
            nc.scalar.preload_act_table_set("natural_log_exp_and_others")
            act.wait_ge(const_in, 16 * 10)
            act.wait_ge(new_scores, 1)
            softplus(nc, act, z[0:TS, 0], t[0:TS, 0]).then_inc(new_logs, 1)
            act.wait_ge(new_carried, 1)
            nc.scalar.activation(a[0:TS, 0], z[0:TS, 0], ACT.Exp).then_inc(new_weights, 1)
            act.wait_ge(new_used, NS)
            act.wait_ge(new_weights, 1)

            def add_bias(x):
                act.wait_ge(scores, x + 1)
                nc.scalar.activation(zb[:].rearrange("r (a k) -> r a k", a=2), zq[:], ACT.Identity,
                                     bias=bias_rows[:, 0:1]).then_inc(biased, 1)

            def log(x, b):
                act.wait_ge(z_turned, x + 1)
                act.wait_ge(plus, x + 1)
                softplus(nc, act, z[:, b], t[:, b]).then_inc(logs, 1)

            def weigh(x, b):
                act.wait_ge(carried, x + 3)
                act.wait_ge(a_taken, x + 1)
                nc.scalar.activation(a[:, b], z[:, b], ACT.Exp).then_inc(exps, 1)

            def round_v(x, i, b):
                act.wait_ge(v_in[b], (i + 1) * (16 * NP))
                act.wait_ge(used, x + 1)
                nc.scalar.copy(v_hi[:, b], vp[:, b]).then_inc(v_rounded, 1)

            add_bias(0)
            log(0, 0)
            round_v(0, 0, 0)
            with act.Fori(0, NX // 2 - 1) as i:
                for b in range(2):
                    weigh(i * 2 + b, b)
                    add_bias(i * 2 + b + 1)
                    log(i * 2 + b + 1, 1 - b)
                    round_v(i * 2 + b + 1, i + b, 1 - b)
            weigh(NX - 2, 0)
            add_bias(NX - 1)
            log(NX - 1, 1)
            round_v(NX - 1, NX // 2 - 1, 1)
            weigh(NX - 1, 1)

        @block.vector
        def _(dve):
            dve.sem_inc(v_read, 2)
            dve.memset(minus[:], -1.0)
            dve.memset(ones_row[:], 1.0)
            dve.memset(qb[:], 0.0)
            dve.memset(carry_in[:], 0.0)
            dve.wait_ge(const_in, 16 * 10)
            dve.wait_ge(proj_in, 16 * 4)
            dve.drain()
            dve.tensor_copy(bias_row[:], bias[:].rearrange("a (p h q) -> a p h q", p=1, q=1)
                            .to_broadcast([1, NP, SBH, TS]))
            dve.tensor_copy(mask_new[:].rearrange("k (n q) -> k n q", q=TS),
                            masked[0:TS, 0:TS].rearrange("k (n q) -> k n q", n=1).to_broadcast([TS, W // TS, TS]))
            for s in range(NS):
                for hh in range(2):
                    r = slice(hh * SBD, (hh + 1) * SBD)
                    for c in range(NC):
                        h = c * 2 + hh
                        dve.tensor_scalar(qb[r, s, c, h * TS:(h + 1) * TS], qn[r, c, s * TS:(s + 1) * TS],
                                          SBD ** -0.5, None, ALU.mult)
            dve.drain()
            dve.sem_inc(ready, 1)
            for two in range(NS // 2):
                dve.wait_ge(turned, two + 1)
                dve.tensor_copy(vt[:, two * 2:two * 2 + 2], vps[0:TS]).then_inc(vt_out, 1)
            dve.wait_ge(new_logs, 1)
            dve.scalar_tensor_tensor(sp[0:TS, 0], z[0:TS, 0], 0.0, t[0:TS, 0], ALU.max, ALU.add)
            dve.drain()
            dve.tensor_tensor(sp[0:TS, 0].rearrange("k (n q) -> k n q", q=TS),
                              sp[0:TS, 0].rearrange("k (n q) -> k n q", q=TS),
                              earlier[0:TS, 0:TS].rearrange("k (n q) -> k n q", n=1).to_broadcast([TS, W // TS, TS]),
                              ALU.mult)
            dve.drain()
            dve.sem_inc(new_plus, 1)
            for s in range(NS):
                dve.tensor_copy(carry_in[0:TS, s], sp[0:TS, 0, s * HQ:(s + 1) * HQ])
            dve.sem_inc(added, 2)
            dve.memset(total[HQ:], 0.0)
            for s in range(NS):
                dve.wait_ge(new_used, s + 1)
                dve.tensor_copy(total[0:HQ, s], out[0:HQ, s % 2]).then_inc(added, 1)
            dve.drain()
            dve.sem_inc(plus, 2)
            dve.sem_inc(a_taken, 2)
            dve.sem_inc(weights, 2)

            def sum_later(x, b):
                dve.wait_ge(logs, x + 1)
                dve.wait_ge(carried, x + 1)
                dve.scalar_tensor_tensor(sp[:, b], z[:, b], 0.0, t[:, b], ALU.max, ALU.add).then_inc(plus, 1)
                dve.tensor_copy(acc[:, b, 0:HQ], carry_in[:, ds(x // NB, 1)].rearrange("p a c -> p (a c)"))
                dve.drain()
                for p in range(NP - 1):
                    ins = dve.tensor_tensor(acc[:, b, (p + 1) * HQ:(p + 2) * HQ], acc[:, b, p * HQ:(p + 1) * HQ],
                                            sp[:, b, p * HQ:(p + 1) * HQ], ALU.add)
                    if p < NP - 2:
                        dve.drain()
                ins.then_inc(summed, 1)
                dve.drain()
                dve.tensor_tensor(carry_in[:, ds(x // NB, 1)].rearrange("p a c -> p (a c)"),
                                  acc[:, b, W - HQ:], sp[:, b, W - HQ:], ALU.add)
                dve.drain()

            def split_v(x, b):
                dve.wait_ge(v_rounded, x + 1)
                dve.wait_ge(used, x + 2)
                dve.tensor_tensor(v_lo[:, 0:VD], vp[:, b, 0:VD], v_hi[:, b, 0:VD].bitcast(F32), ALU.subtract
                                  ).then_inc(v_split, 1)
                dve.drain()
                dve.sem_inc(v_read, 1)

            def split_a(x, b):
                dve.wait_ge(exps, x + 1)
                dve.wait_ge(used, x + 1)
                a_b = a[:, b].rearrange("k (p r) -> k p r", p=NP)
                dve.tensor_copy(a_pair[:, b, :, 0], a_b)
                dve.drain()
                dve.tensor_tensor(a_pair[:, b, :, 1], a_b, a_pair[:, b, :, 0].bitcast(F32), ALU.subtract
                                  ).then_inc(weights, 1)
                dve.drain()
                dve.sem_inc(a_taken, 1)

            def add(x, b):
                s = ds(x // NB, 1)
                dve.wait_ge(used, x + 3)
                dve.tensor_tensor(total[:, s], out[:, b:b + 1], total[:, s], ALU.add).then_inc(added, 1)
                dve.drain()

            def set_q(x, b):
                dve.wait_ge(scores, x - 1)
                dve.tensor_copy(q_now[:, b:b + 1], qb[:, ds(x // NB, 1)]).then_inc(q_set, 1)

            for b in range(2):
                dve.tensor_copy(q_now[:, b], qb[:, 0]).then_inc(q_set, 1)
            sum_later(0, 0)
            with dve.Fori(0, NX // 2 - 1) as i:
                for b in range(2):
                    set_q(i * 2 + b + 2, b)
                    split_v(i * 2 + b, b)
                    split_a(i * 2 + b, b)
                    sum_later(i * 2 + b + 1, 1 - b)
                    add(i * 2 + b, b)
            split_v(NX - 2, 0)
            split_a(NX - 2, 0)
            sum_later(NX - 1, 1)
            add(NX - 2, 0)
            split_v(NX - 1, 1)
            split_a(NX - 1, 1)
            add(NX - 1, 1)
            for s in range(NS):
                dve.tensor_tensor(total[:, s], total[:, s], heads[:], ALU.mult)
            dve.drain()
            dve.sem_inc(masked_out, 1)
            dve.wait_ge(turned, NS // 2 + 1)
            dve.tensor_tensor(o[:], vps[:, 0, 0:NC * NS * TS].rearrange("p (c t) -> p c t", c=NC), zn[:],
                              ALU.mult).then_inc(new_done, 1)
def gdn(nc, name, proj, qkv, rate_dram, out_w_dram, const_dram, own_dram, state_dram, mix, new_state, new_states):
    NCH = SEQ // P
    H = GH
    with Stage(nc, name) as st:
        mat = lambda s: st.sb(s, [P, 2, H, P])
        col = lambda s: st.sb(s, [P, 2, H])
        x = st.sb("x", [P, 2, 3 * H, P])
        gate = st.sb("gate", [P, 2, H, P])
        ba = st.sb("ba", [2 * H, T])
        rate = st.sb("rate", [P, 2 * H])
        out_w = st.sb("out_w", [P, 1])
        beta, g, tmp = (st.sb(s, [P, NCH + 2, H]) for s in ("beta", "g", "tmp"))
        g_now, beta_now, minus_beta, gc, egc, k_scale, kd_scale, ss, rstd = (
            col(s) for s in ("g_now", "beta_now", "minus_beta", "gc", "egc", "k_scale", "kd_scale", "ss", "rstd"))
        consts = {s: st.sb(s, [P, P]) for s in CONST if s not in ("suffix", "earlier", "not_earlier")}
        own_row = st.sb("own_row", [P, NS])
        ones, eps = st.sb("ones", [P, P]), st.sb("eps", [P, 1])
        gu, eg, dec, kk, qk, n, nb, nbt, y, r, yt = (mat(s) for s in (
            "gu", "eg", "dec", "kk", "qk", "n", "nb", "nbt", "y", "r", "yt"))
        p2, p2t, p4, p4t, p8 = (mat(s) for s in ("p2", "p2t", "p4", "p4t", "p8"))
        joins = [mat(f"join{l}") for l in (16, 32, 64)]
        vb, kbg, kd, qg, wn, vnew, on, o = (mat(s) for s in ("vb", "kbg", "kd", "qg", "wn", "vnew", "on", "o"))
        state = st.sb("state", [P, H, P])
        states = st.sb("states", [P, NS, H, P])
        w_own, q_own = (st.sb(s, [P, H, NS * (P + TS)]) for s in ("w_own", "q_own"))
        kd_own = st.sb("kd_own", [P, H, NS, P])
        bank = [st.psum(f"bank{j}", [P, H, P]) for j in range(6)]
        small = st.psum("small", [P, 2, 512])
        x_in = [st.sem(f"x_in{b}") for b in range(2)]
        const_in, ba_in, state_in, const_set = (st.sem(s) for s in ("const_in", "ba_in", "state_in", "const_set"))
        gate_in = [st.sem(f"gate_in{b}") for b in range(2)]
        stored = [st.sem(f"stored{b}") for b in range(2)]
        ba_turned, ba_exp = st.sem("ba_turned"), st.sem("ba_exp")
        x_read, gate_read = st.sem("x_read"), st.sem("gate_read")
        states_stored = st.sem("states_stored")
        PE = ["rows", "scores", "turned", "n_turned", "square2", "square4", "square8", "y8",
              "join0", "grow0", "join1", "grow1", "join2", "grow2", "w", "v_new", "out", "o_turned"]
        DV = ["decay_log", "m", "n", "y1", "y2", "y4", "y8", "y16", "y32", "y64", "state", "o"]
        AC = ["eg", "decay", "keys", "p2", "p4", "p8", "r0", "r1", "r2", "w", "v_new", "on"]
        PO = ["gu", "joins"]
        pe_step, dve_step, act_step, pool_step = (st.sem(s) for s in ("pe_step", "dve_step", "act_step", "pool_step"))
        now_set, scales = st.sem("now_set"), st.sem("scales")
        begun = st.sem("begun")

        def count(names, late):
            k = names.index(late) if late else len(names)

            def value(pair, width, b, s):
                j = names.index(s)
                at = j * width + b if j < k else k * width + b * (len(names) - k) + j - k
                return pair * (2 * len(names)) + at + 1
            return value
        at_pe, at_dve, at_act, at_pool = count(PE, "v_new"), count(DV, "state"), count(AC, "v_new"), count(PO, None)
        block = st.block()
        heads = range(H)
        OWN_BANKS = (0, 3, 4, 5)

        def four(m):
            return m[:].rearrange("p (h c) -> p h c", h=1).to_broadcast([P, H, P])

        def pairs(eng, body):
            with eng.Fori(0, NCH // 2) as i:
                body(i, (0, 1), False)
            body(NCH // 2, (0,), True)

        @block.sync
        def _(sp):
            for s in consts:
                sp.dma_start(consts[s][:], const(const_dram, s)).then_inc(const_in, 16)
            for dst, src in ((rate, rate_dram), (out_w, out_w_dram), (own_row, own_dram)):
                sp.dma_start(dst[:], src).then_inc(const_in, 16)
            sp.dma_start(ba[:], proj[BA0 * P:BA0 * P + 2 * H]).then_inc(ba_in, 16)
            for s in range(NS):
                sp.dma_start(states[:, s], state_dram[s].rearrange("h k v -> k h v")).then_inc(state_in, 16)

            def columns(i, b, own):
                return (slice(SEQ, T), NS * TS) if own else (ds((i * 2 + b) * P, P), P)

            def load_x(i, pair, own=False):
                for b in pair:
                    cols, wide = columns(i, b, own)
                    sp.wait_ge(x_read, i * 2 + b + 1)
                    sp.dma_start(x[:, b, :, 0:wide], qkv[:, cols].rearrange("(m p) t -> p m t", p=P)).then_inc(x_in[b], 16)

            def load_gate(i, pair, own=False):
                for b in pair:
                    cols, wide = columns(i, b, own)
                    sp.wait_ge(gate_read, i * 2 + b + 1)
                    sp.dma_start(gate[:, b, :, 0:wide], proj[GZ0 * P:(GZ0 + H) * P, cols].rearrange(
                        "(m p) t -> p m t", p=P)).then_inc(gate_in[b], 16)

            def store(i, pair, own=False):
                for b in pair:
                    cols, wide = columns(i, b, own)
                    sp.wait_ge(dve_step, at_dve(i, len(pair), b, "o"))
                    sp.dma_start(mix[SBH * SBD:, cols].rearrange("(m p) t -> p m t", p=P), o[:, b, :, 0:wide]
                                 ).then_inc(stored[b], 16)

            for b in range(2):
                sp.sem_inc(stored[b], 16)
            load_x(0, (0, 1))
            load_gate(0, (0, 1))
            with sp.Fori(0, NCH // 2 - 1) as i:
                load_x(i + 1, (0, 1))
                store(i, (0, 1))
                load_gate(i + 1, (0, 1))
            load_x(NCH // 2, (0,), True)
            store(NCH // 2 - 1, (0, 1))
            load_gate(NCH // 2, (0,), True)
            store(NCH // 2, (0,), True)
            sp.wait_ge(stored[0], 16 * (NCH // 2 + 2))
            sp.wait_ge(stored[1], 16 * (NCH // 2 + 1))

        @block.gpsimd
        def _(pool):
            pool.wait_ge(const_set, 1)
            pool.wait_ge(const_in, 16 * (len(consts) + 3))

            def body(i, pair, own):
                upto = consts["upto_own" if own else "upto"]
                pool.wait_ge(now_set, i + 1)
                for b in pair:
                    pool.tensor_tensor(gu[:, b], upto[:].rearrange("p (h c) -> p h c", h=1).to_broadcast([P, H, P]),
                                       g_now[:, b].rearrange("p (h c) -> p h c", c=1).to_broadcast([P, H, P]),
                                       ALU.mult).then_inc(pool_step, 1)
                for b in pair:
                    pool.wait_ge(dve_step, at_dve(i, len(pair), b, "n"))
                    for l, s in enumerate((16, 32, 64)):
                        ins = pool.tensor_tensor(joins[l][:, b], n[:, b], four(consts[f"level{s}"]), ALU.mult)
                    ins.then_inc(pool_step, 1)
            pairs(pool, body)
            pool.wait_ge(dve_step, at_dve(NCH // 2, 1, 0, "o"))
            pool.dma_start(new_state.rearrange("h k v -> k h v"), state[:]).then_inc(states_stored, 16)
            for s in range(NS):
                pool.dma_start(new_states[s].rearrange("h k v -> k h v"), states[:, s]).then_inc(states_stored, 16)
            pool.wait_ge(states_stored, 16 * (NS + 1))

        @block.tensor
        def _(pe):
            ident = consts["ident"]
            pe.wait_ge(const_in, 16 * (len(consts) + 3))
            pe.wait_ge(ba_in, 16)
            pe.wait_ge(const_set, 1)
            for c in range(NCH + 1):
                wide = P if c < NCH else NS * TS
                mm = pe.transpose(small[0:wide, 0, c * 2 * H:(c + 1) * 2 * H], ba[:, c * P:c * P + wide],
                                  ident[0:2 * H, 0:2 * H])
            mm.then_inc(ba_turned, 1)

            def each(out, lhs, rhs):
                for h in heads:
                    mm = pe.matmul(out[:, h], lhs[:, h], rhs[:, h], start=True, stop=True)
                return mm

            def turn(out, src):
                for h in heads:
                    mm = pe.transpose(out[:, h], src[:, h], ident[:])
                return mm

            def body(i, pair, own):
                width = len(pair)
                dve = lambda b, s: pe.wait_ge(dve_step, at_dve(i, width, b, s))
                act = lambda b, s: pe.wait_ge(act_step, at_act(i, width, b, s))
                pool = lambda b, s: pe.wait_ge(pool_step, at_pool(i, width, b, s))
                A, B, C = ([bank[3 * b + j] for b in range(2)] for j in range(3))
                upto = consts["upto_own" if own else "upto"]
                pe.wait_ge(begun, i + 1)
                for b in pair:
                    pool(b, "gu")
                    pe.matmul(A[b][:].rearrange("p h c -> p (h c)"), ones[:], gu[:, b].rearrange("p h c -> p (h c)"),
                              start=True, stop=True)
                    pe.matmul(small[:, b, 0:H], upto[:], g_now[:, b], start=True, stop=True
                              ).then_inc(pe_step, 1)
                for b in pair:
                    q, k = x[:, b, 0:3 * H:3], x[:, b, 1:3 * H:3]
                    pe.wait_ge(x_in[b], i * 16 + 16)
                    each(B[b], k, k)
                    each(C[b], k, q).then_inc(pe_step, 1)
                for b in pair:
                    dve(b, "m")
                    turn(C[b], kk[:, b])
                    turn(A[b], x[:, b, 1:3 * H:3])
                    turn(B[b], x[:, b, 2:3 * H:3]).then_inc(pe_step, 1)
                for b in pair:
                    dve(b, "n")
                    turn(C[b], n[:, b]).then_inc(pe_step, 1)
                for b in pair:
                    act(b, "keys")
                    dve(b, "y1")
                    each(A[b], nbt[:, b], nb[:, b])
                    each(B[b], nb[:, b], nbt[:, b]).then_inc(pe_step, 1)
                for b in pair:
                    act(b, "p2")
                    each(C[b], p2[:, b], y[:, b])
                    each(A[b], p2t[:, b], p2[:, b])
                    each(B[b], p2[:, b], p2t[:, b]).then_inc(pe_step, 1)
                for b in pair:
                    act(b, "p4")
                    dve(b, "y2")
                    each(A[b], p4t[:, b], p4[:, b])
                    each(C[b], p4[:, b], y[:, b]).then_inc(pe_step, 1)
                for b in pair:
                    act(b, "p8")
                    dve(b, "y4")
                    each(C[b], p8[:, b], y[:, b]).then_inc(pe_step, 1)
                for l, ready in enumerate(("y8", "y16", "y32")):
                    for b in pair:
                        dve(b, ready)
                        if l == 0:
                            pool(b, "joins")
                        each(A[b], joins[l][:, b], y[:, b])
                        turn(B[b], y[:, b]).then_inc(pe_step, 1)
                    for b in pair:
                        act(b, f"r{l}")
                        each(C[b], yt[:, b], r[:, b]).then_inc(pe_step, 1)
                for b in pair:
                    dve(b, "y64")
                    each(A[b], kbg[:, b], y[:, b]).then_inc(pe_step, 1)
                for b in pair:
                    act(b, "w")
                    for h in heads:
                        pe.matmul(B[b][:, h], y[:, b, h], vb[:, b, h], start=True, stop=False)
                        if not own:
                            if b and h == 0:
                                dve(0, "state")
                            elif h == 0:
                                pe.wait_ge(begun, i + 1)
                            mm = pe.matmul(B[b][:, h], wn[:, b, h], state[:, h], start=False, stop=True)
                        else:
                            for s in range(NS):
                                mm = pe.matmul(B[b][:, h], w_own[:, h, s * P:(s + 1) * P], states[:, s, h],
                                               start=False, stop=(s == NS - 1))
                    mm.then_inc(pe_step, 1)
                    act(b, "v_new")
                    for h in heads:
                        if not own:
                            pe.matmul(C[b][:, h], qg[:, b, h], state[:, h], start=True, stop=False)
                        else:
                            for s in range(NS):
                                pe.matmul(C[b][:, h], q_own[:, h, s * P:(s + 1) * P], states[:, s, h],
                                          start=(s == 0), stop=False)
                        pe.matmul(C[b][:, h], qk[:, b, h], vnew[:, b, h], start=False, stop=True)
                    if not own:
                        mm = each(A[b], kd[:, b], vnew[:, b])
                    else:
                        for s in range(4):
                            for h in heads:
                                mm = pe.matmul(bank[OWN_BANKS[s]][:, h], kd_own[:, h, s], vnew[:, b, h],
                                               start=True, stop=True)
                    mm.then_inc(pe_step, 1)
                    act(b, "on")
                    turn(B[b], on[:, b]).then_inc(pe_step, 1)
                if own:
                    dve(0, "state")
                    for s in range(4, NS):
                        for h in heads:
                            mm = pe.matmul(bank[OWN_BANKS[s - 4]][:, h], kd_own[:, h, s], vnew[:, 0, h],
                                           start=True, stop=True)
                    mm.then_inc(pe_step, 1)
            pairs(pe, body)

        @block.scalar
        def _(act):
            nc.scalar.preload_act_table_set("natural_log_exp_and_others")
            act.wait_ge(const_in, 16 * (len(consts) + 3))
            act.wait_ge(const_set, 1)
            act.wait_ge(ba_exp, 1)
            nc.scalar.activation(beta[:], beta[:], ACT.Exp, scale=-1.0)
            nc.scalar.activation(rate[:, 0:H], rate[:, 0:H], ACT.Exp)
            softplus(nc, act, g[:], tmp[:]).then_inc(ba_exp, 1)
            copy = nc.scalar.copy

            def body(i, pair, own):
                pe = lambda b, s: act.wait_ge(pe_step, at_pe(i, len(pair), b, s))
                dve = lambda b, s: act.wait_ge(dve_step, at_dve(i, len(pair), b, s))
                A, B, C = ([bank[3 * b + j] for b in range(2)] for j in range(3))
                for b in pair:
                    pe(b, "rows")
                    nc.scalar.activation(eg[:, b], A[b][:], ACT.Exp).then_inc(act_step, 1)
                for b in pair:
                    dve(b, "decay_log")
                    nc.scalar.activation(egc[:, b], gc[:, b], ACT.Exp)
                    nc.scalar.activation(dec[:, b], dec[:, b], ACT.Exp).then_inc(act_step, 1)
                for b in pair:
                    act.wait_ge(scales, i * 2 + b + 1)
                    pe(b, "turned")
                    for h in heads:
                        nc.scalar.activation(kbg[:, b, h], A[b][:, h], ACT.Copy, scale=k_scale[:, b, h:h + 1])
                        nc.scalar.activation(kd[:, b, h], A[b][:, h], ACT.Copy, scale=kd_scale[:, b, h:h + 1])
                        ins = nc.scalar.activation(vb[:, b, h], B[b][:, h], ACT.Copy, scale=beta_now[:, b, h:h + 1])
                    ins.then_inc(act_step, 1)
                for b in pair:
                    pe(b, "square2")
                    copy(p2[:, b], A[b][:])
                    copy(p2t[:, b], B[b][:]).then_inc(act_step, 1)
                for b in pair:
                    pe(b, "square4")
                    copy(p4[:, b], A[b][:])
                    copy(p4t[:, b], B[b][:]).then_inc(act_step, 1)
                for b in pair:
                    pe(b, "square8")
                    copy(p8[:, b], A[b][:]).then_inc(act_step, 1)
                for l in range(3):
                    for b in pair:
                        pe(b, f"join{l}")
                        copy(r[:, b], A[b][:])
                        copy(yt[:, b], B[b][:]).then_inc(act_step, 1)
                for b in pair:
                    pe(b, "w")
                    if not own:
                        nc.scalar.mul(wn[:, b], A[b][:], -1.0).then_inc(act_step, 1)
                    else:
                        for h in heads:
                            mm = nc.scalar.mul(w_own[:, h].rearrange("p (s t) -> p s t", s=NS)[:, :, 0:TS],
                                               A[b][:, h, 0:NS * TS].rearrange("p (s t) -> p s t", s=NS), -1.0)
                        mm.then_inc(act_step, 1)
                for b in pair:
                    pe(b, "v_new")
                    copy(vnew[:, b], B[b][:]).then_inc(act_step, 1)
                    pe(b, "out")
                    for h in heads:
                        nc.scalar.activation(on[:, b, h], C[b][:, h], ACT.Square, accum_out=ss[:, b, h:h + 1])
                    act.drain()
                    nc.scalar.activation(ss[:, b], ss[:, b], ACT.Ln, scale=1.0 / P, bias=eps[:, 0:1])
                    act.drain()
                    nc.scalar.activation(rstd[:, b], ss[:, b], ACT.Exp, scale=-0.5)
                    act.drain()
                    for h in heads:
                        ins = nc.scalar.activation(on[:, b, h], C[b][:, h], ACT.Copy, scale=rstd[:, b, h:h + 1])
                    ins.then_inc(act_step, 1)
            pairs(act, body)

        @block.vector
        def _(dve):
            dve.memset(ones[:], 1.0)
            dve.memset(eps[:], EPS)
            for s in (beta, g, tmp, state, w_own, q_own, ss, x, gate):
                dve.memset(s[:], 0.0)
            dve.drain()
            dve.sem_inc(const_set, 1)
            dve.sem_inc(x_read, 2)
            dve.sem_inc(gate_read, 2)
            dve.wait_ge(const_in, 16 * (len(consts) + 3))
            dve.wait_ge(state_in, 16 * NS)
            dve.wait_ge(ba_turned, 1)
            turned = small[:, 0, 0:(NCH + 1) * 2 * H].rearrange("p (c a h) -> p c a h", a=2, h=H)
            full, part = (slice(0, P), slice(0, NCH)), (slice(0, NS * TS), slice(NCH, NCH + 1))
            for rows, cs in (full, part):
                dve.tensor_copy(beta[rows, cs], turned[rows, cs, 0])
                dt = rate[rows, H:].rearrange("p (c h) -> p c h", c=1).to_broadcast([rows.stop, cs.stop - cs.start, H])
                dve.tensor_tensor(g[rows, cs], turned[rows, cs, 1], dt, ALU.add)
            dve.drain()
            dve.sem_inc(ba_exp, 1)
            dve.wait_ge(ba_exp, 2)
            dve.tensor_scalar(beta[:], beta[:], 1.0, None, ALU.add)
            dve.scalar_tensor_tensor(g[:], g[:], 0.0, tmp[:], ALU.max, ALU.add)
            dve.drain()
            dve.reciprocal(beta[:], beta[:])
            a = rate[:, 0:H].rearrange("p (c h) -> p c h", c=1).to_broadcast([P, NCH + 2, H])
            dve.scalar_tensor_tensor(g[:], g[:], -1.0, a, ALU.mult, ALU.mult)
            dve.drain()
            dve.memset(beta[NS * TS:, NCH], 0.0)
            dve.memset(g[NS * TS:, NCH], 0.0)
            dve.drain()

            def set_now(i):
                dve.tensor_copy(g_now[:], g[:, ds(i * 2, 2)])
                dve.tensor_copy(beta_now[:], beta[:, ds(i * 2, 2)])
                dve.tensor_scalar(minus_beta[:], beta[:, ds(i * 2, 2)], -1.0, None, ALU.mult)
                dve.drain()
                dve.sem_inc(now_set, 1)

            set_now(0)

            def body(i, pair, own):
                pe = lambda b, s: dve.wait_ge(pe_step, at_pe(i, len(pair), b, s))
                act = lambda b, s: dve.wait_ge(act_step, at_act(i, len(pair), b, s))
                A, B, C = ([bank[3 * b + j] for b in range(2)] for j in range(3))
                later = consts["later_own" if own else "later"]
                tt, ts = dve.tensor_tensor, dve.tensor_scalar
                dve.sem_inc(begun, 1)
                for b in pair:
                    act(b, "eg")
                    dve.tensor_copy(gc[:, b], small[:, b, 0:H])
                    dve.drain()
                    for h in heads:
                        ins = dve.scalar_tensor_tensor(dec[:, b, h], A[b][:, h], gc[:, b, h:h + 1], later[:],
                                                       ALU.subtract, ALU.add)
                    ins.then_inc(dve_step, 1)
                for b in pair:
                    act(b, "decay")
                    pe(b, "scores")
                    tt(kk[:, b], B[b][:], dec[:, b], ALU.mult)
                    tt(qk[:, b], C[b][:], dec[:, b], ALU.mult)
                    dve.drain()
                    dve.sem_inc(dve_step, 1)
                    tt(k_scale[:, b], beta_now[:, b], egc[:, b], ALU.mult)
                    if not own:
                        dve.tensor_copy(kd_scale[:, b], dec[:, b, :, P - 1])
                    else:
                        dve.tensor_reduce(kd_scale[:, b], dec[:, b, :, TS - 1:NS * TS:TS], mybir.AxisListType.X,
                                          ALU.add)
                    dve.drain()
                    dve.sem_inc(scales, 1)
                for b in pair:
                    pe(b, "turned")
                    tt(n[:, b], C[b][:], minus_beta[:, b].rearrange("p (h c) -> p h c", c=1).to_broadcast([P, H, P]),
                       ALU.mult).then_inc(dve_step, 1)
                    dve.drain()
                    tt(nb[:, b], n[:, b], four(consts["low16"]), ALU.mult)
                for b in pair:
                    pe(b, "n_turned")
                    tt(nbt[:, b], C[b][:], four(consts["up16"]), ALU.mult)
                    dve.drain()
                    tt(y[:, b], nbt[:, b], four(consts["ident"]), ALU.add).then_inc(dve_step, 1)
                    dve.drain()
                for b in pair:
                    tt(qg[:, b], x[:, b, 0:3 * H:3], eg[:, b], ALU.mult)
                    dve.drain()
                    dve.sem_inc(x_read, 1)
                    if own:
                        for h in heads:
                            dve.tensor_copy(q_own[:, h].rearrange("p (s t) -> p s t", s=NS)[:, :, 0:TS],
                                            qg[:, b, h, 0:NS * TS].rearrange("p (s t) -> p s t", s=NS))
                if own:
                    act(0, "keys")
                    for h in heads:
                        for s in range(NS):
                            ts(kd_own[:, h, s], kd[:, 0, h], own_row[:, s:s + 1], None, ALU.mult)
                for product in ("square4", "square8", "y8", "grow0", "grow1", "grow2"):
                    for b in pair:
                        pe(b, product)
                        tt(y[:, b], C[b][:], y[:, b], ALU.add).then_inc(dve_step, 1)
                        dve.drain()

                if not own:
                    set_now(i + 1)

                def grow_states(samples):
                    for s in samples:
                        for h in heads:
                            last = s * TS + TS - 1
                            dve.scalar_tensor_tensor(states[:, s, h], states[:, s, h], eg[:, 0, h, last:last + 1],
                                                     bank[OWN_BANKS[s % 4]][:, h], ALU.mult, ALU.add)
                for b in pair:
                    pe(b, "out")
                    if not own:
                        for h in heads:
                            dve.scalar_tensor_tensor(state[:, h], state[:, h], eg[:, b, h, P - 1:P], A[b][:, h],
                                                     ALU.mult, ALU.add)
                    else:
                        grow_states(range(4))
                    dve.drain()
                    dve.sem_inc(dve_step, 1)
                    pe(b, "o_turned")
                    if own:
                        dve.wait_ge(pe_step, at_pe(i, 1, 0, "o_turned") + 1)
                        grow_states(range(4, NS))
                    dve.wait_ge(stored[b], i * 16 + 16)
                    dve.wait_ge(gate_in[b], i * 16 + 16)
                    dve.scalar_tensor_tensor(o[:, b], B[b][:], out_w[:, 0:1], gate[:, b], ALU.mult, ALU.mult)
                    dve.drain()
                    dve.sem_inc(dve_step, 1)
                    dve.sem_inc(gate_read, 1)
            pairs(dve, body)
def hybrid_step(nc, i, o, scratch):
    with nc.sbuf_tensor("xh", [P, KC, T], F32R) as xh, nc.sbuf_tensor("xl", [P, KC, T], F32R) as xl:
        norm(nc, "norm0", i["x"], i["norm_w0"], xh, xl, None)
        project(nc, "proj", i["w_in"], Z0, xh, xl, o["proj"][0:Z0 * P])
        project(nc, "gates", i["w_gates"], NROW - Z0, xh, xl, o["proj"][Z0 * P:], silu=True)
        project_gdn(nc, "projg", i["w_gdn"], i["par_gdn"], xh, xl, scratch["qkv"], o["tail_gdn"])
    prompt_attention(nc, "pattn", o["proj"], i["sb_bias"], i["const"], scratch["mix"])
    sample_attention(nc, "sattn", o["proj"], i["sb_bias"], i["sb_bias_rows"], i["pages"], i["k_pool"], i["v_pool"],
                     i["const"], i["head_const"], scratch["mix"])
    gdn(nc, "gdn", o["proj"], scratch["qkv"], i["rate"], i["out_norm_w"], i["const"], i["own_rows"], i["state"],
        scratch["mix"], o["new_state"], o["new_states"])
    with nc.sbuf_tensor("yh", [P, KC, T], F32R) as xh, nc.sbuf_tensor("yl", [P, KC, T], F32R) as xl:
        split(nc, "split0", scratch["mix"], xh, xl)
        project(nc, "out0", i["w_out0"], KC, xh, xl, scratch["h1"], residual=i["x"])
        norm(nc, "norm1", scratch["h1"], i["norm_w1"], xh, xl, None)
        shortconv(nc, "sconv", i["w_sc"], i["par_sc"], xh, xl, scratch["mix"], o["tail_sc"])
        split(nc, "split1", scratch["mix"], xh, xl)
        project(nc, "out1", i["w_out1"], KC, xh, xl, scratch["h2"], residual=scratch["h1"])
    norm(nc, "norm2", scratch["h2"], i["norm_w2"], None, None, o["y"])


def _blocks(w, order=None):
    w = np.pad(w, ((0, 0), (0, -w.shape[1] % P)))
    w = w.reshape(KC, P, -1, P).transpose(2, 1, 0, 3)
    return np.ascontiguousarray(w if order is None else w[order])


def _params(past, taps):
    n, t, c = past.shape
    return np.ascontiguousarray(np.concatenate([past.transpose(2, 0, 1).reshape(c, n * t), taps.T], 1))


GDN_ORDER = [part * GH + h for h in range(GH) for part in range(3)]
SC_ORDER = [part * KC + j for j in range(KC) for part in range(4)]


def kernel(x_prompt, x_sample, cache_sb_k, cache_sb_v, state_gdn, state_gdn_conv, state_sconv, page_table,
           norm_w, ab_w_in, ab_sb_bias, ab_conv_w, ab_a_log, ab_dt_bias, ab_out_norm_w, ab_w_out,
           sc_w_in, sc_conv_w, sc_w_out, final_norm_w):
    import concourse.bacc as _bacc
    from concourse.bass_utils import run_bass_kernel_spmd as _run

    a = np.asarray
    npool = cache_sb_k.shape[1]
    w_in = a(ab_w_in)[0]
    sbw, gw = 4 * SBH * SBD, 3 * GH * P
    col = lambda w: np.ascontiguousarray(a(w).reshape(KC, P).T)
    arrays = {
        "x": np.ascontiguousarray(np.concatenate([a(x_prompt).reshape(SEQ, D), a(x_sample).reshape(NS * TS, D)]).T),
        "norm_w0": col(norm_w[0]), "norm_w1": col(norm_w[1]), "norm_w2": col(final_norm_w),
        "w_in": _blocks(np.concatenate([w_in[:, :3 * SBH * SBD], w_in[:, sbw + gw + GH * P:]], 1)),
        "w_gates": _blocks(np.concatenate([w_in[:, 3 * SBH * SBD:sbw], w_in[:, sbw + gw:sbw + gw + GH * P]], 1)),
        "w_gdn": _blocks(w_in[:, sbw:sbw + gw], GDN_ORDER),
        "par_gdn": np.ascontiguousarray(
            _params(a(state_gdn_conv)[0], a(ab_conv_w)[0]).reshape(3 * GH, P, -1)[GDN_ORDER].reshape(gw, -1)),
        "sb_bias": a(ab_sb_bias), "sb_bias_rows": np.repeat(a(ab_sb_bias)[0], TS)[:, None],
        "const": constants(), "head_const": head_constants(), "own_rows": own_rows(),
        "pages": np.ascontiguousarray(a(page_table)[:, ::-1]).reshape(1, -1),
        "k_pool": np.ascontiguousarray(a(cache_sb_k)[0].reshape(npool, PAGE, SBH // 2, 2, SBD).transpose(0, 3, 4, 2, 1)
                                       ).reshape(npool, P, SBH // 2, PAGE),
        "v_pool": a(cache_sb_v)[0].reshape(npool, PAGE, SBH * SBD),
        "rate": np.repeat(np.concatenate([a(ab_a_log), a(ab_dt_bias)], 1), P, 0),
        "out_norm_w": np.ascontiguousarray(a(ab_out_norm_w).T),
        "state": a(state_gdn)[0],
        "w_out0": _blocks(a(ab_w_out)[0]),
        "w_sc": _blocks(a(sc_w_in)[0], SC_ORDER),
        "par_sc": _params(a(state_sconv)[0], a(sc_conv_w)[0]),
        "w_out1": _blocks(a(sc_w_out)[0]),
    }
    outs = {"proj": (NROW * P, T), "tail_gdn": (gw, 3 * (1 + NS)), "tail_sc": (D, 2 * (1 + NS)), "y": (D, T),
            "new_state": (GH, P, P), "new_states": (NS, GH, P, P)}
    temps = {"qkv": (gw, T), "mix": (D, T), "h1": (D, T), "h2": (D, T)}

    nc = _bacc.Bacc("TRN2", target_bir_lowering=False, num_devices=1)
    dram = lambda n, s, dt, kind: nc.dram_tensor(n, s, dt, kind=kind).ap()
    i = {n: dram(f"in_{n}", v.shape, mybir.dt.from_np(v.dtype), "ExternalInput") for n, v in arrays.items()}
    o = {n: dram(f"out_{n}", s, F32, "ExternalOutput") for n, s in outs.items()}
    scratch = {n: dram(f"tmp_{n}", s, F32, "Internal") for n, s in temps.items()}
    hybrid_step(nc, i, o, scratch)
    r = _run(nc, [{f"in_{n}": v for n, v in arrays.items()}], core_ids=[0]).results[0]
    r = {n: r[f"out_{n}"] for n in outs}

    def rows(m, prompt):
        return m[:, :SEQ].T[None] if prompt else m[:, SEQ:].T.reshape(NS, TS, -1)

    kv = [[rows(r["proj"][b * P:(b + 4) * P], p) for b in (K0, V0)] for p in (True, False)]
    kv = [[m.reshape(1, *m.shape[:2], SBH, SBD) for m in pair] for pair in kv]

    def tails(m, width):
        return m[:, :width].T[None, None], m[:, width:].reshape(-1, NS, width).transpose(1, 2, 0)[None]

    back = np.argsort(GDN_ORDER)
    gp, gs = tails(r["tail_gdn"].reshape(3 * GH, P, -1)[back].reshape(gw, -1), 3)
    sp, ss = tails(r["tail_sc"], 2)
    c = np.ascontiguousarray
    return (c(rows(r["y"], True)), c(rows(r["y"], False)), c(kv[0][0]), c(kv[0][1]), c(kv[1][0]), c(kv[1][1]),
            r["new_state"][None, None], r["new_states"][None], c(gp), c(gs), c(sp), c(ss))
```
